# Optimizing a Trainium2 kernel written in Bass

```python
import functools
import jax, jax.numpy as jnp
from jax import lax
import numpy as np

D_MODEL = 1024
BATCH = 1
SEQ = 512
DEPTH = 1
DEC_BATCH = 1
DEC_SEQ = 32
PAST_LEN = 512

CHUNK = 64
LEFT_CHUNKS = 8
BAND_LEFT = LEFT_CHUNKS * CHUNK
BAND = BAND_LEFT + CHUNK
N_HEADS_A = 8
HEAD_DIM_A = 64
D_ATTN = N_HEADS_A * HEAD_DIM_A
REL_CLIP = 128
N_REL = REL_CLIP + CHUNK
N_HEADS_B = 8
HEAD_DIM_B = 64
D_RWKV = N_HEADS_B * HEAD_DIM_B
DECAY_RANK = 64
ICLR_RANK = 64
GATE_RANK = 128
SHIFT_COLS = 3 * D_RWKV + DECAY_RANK + ICLR_RANK + GATE_RANK
N_BRANCH = 2
PROJ_COLS = 3 * D_ATTN + SHIFT_COLS + N_BRANCH * D_MODEL
D_FF = -(-8 * D_MODEL // (3 * 256)) * 256
RMS_EPS = 1e-6
GN_EPS = 64e-5
NEG_INF = -1e30

kernel_name = 'chunk_hybrid_stream_step'

def rmsnorm(x, g):
    xf = x.astype(jnp.float32)
    y = xf * lax.rsqrt(jnp.mean(xf * xf, axis=-1, keepdims=True) + RMS_EPS)
    return (y * g.astype(jnp.float32)).astype(x.dtype)

def band_attend(q, k, v, q_pos, k_pos, valid, rel_bias):
    idx = jnp.clip(k_pos[None, :] - q_pos[:, None], -REL_CLIP, CHUNK - 1) + REL_CLIP
    bias = rel_bias[:, idx].astype(jnp.float32)
    s = jnp.einsum('bqhd,bkhd->bhqk', q, k).astype(jnp.float32) * (HEAD_DIM_A ** -0.5) + bias[None]
    s = jnp.where(valid[None, None, None, :], s, NEG_INF)
    p = jax.nn.softmax(s, axis=-1)
    return jnp.einsum('bhqk,bkhd->bqhd', p.astype(v.dtype), v)

def chunk_band_attention(q, k, v, rel_bias):
    B, T, H, Dh = q.shape
    nc = T // CHUNK
    pad = ((0, 0), (BAND_LEFT, 0), (0, 0), (0, 0))
    kp, vp = jnp.pad(k, pad), jnp.pad(v, pad)
    qc = jnp.moveaxis(q.reshape(B, nc, CHUNK, H, Dh), 1, 0)

    def one_chunk(args):
        q_c, ci = args
        start = ci * CHUNK
        kb = lax.dynamic_slice_in_dim(kp, start, BAND, axis=1)
        vb = lax.dynamic_slice_in_dim(vp, start, BAND, axis=1)
        q_pos = start + jnp.arange(CHUNK)
        k_pos = start - BAND_LEFT + jnp.arange(BAND)
        return band_attend(q_c, kb, vb, q_pos, k_pos, k_pos >= 0, rel_bias)

    o = lax.map(one_chunk, (qc, jnp.arange(nc)))
    return jnp.moveaxis(o, 0, 1).reshape(B, T, H, Dh)

def cached_band_attention(q, k, v, rel_bias, k_cache, v_cache):
    Ts = q.shape[1]
    Wc = k_cache.shape[1]
    kb = jnp.concatenate([k_cache.astype(k.dtype), k], axis=1)
    vb = jnp.concatenate([v_cache.astype(v.dtype), v], axis=1)
    q_pos = PAST_LEN + jnp.arange(Ts)
    k_pos = jnp.concatenate([PAST_LEN - Wc + jnp.arange(Wc), q_pos])
    valid = jnp.ones((Wc + Ts,), dtype=bool)
    return band_attend(q, kb, vb, q_pos, k_pos, valid, rel_bias)

def wkv7_scan(r, decay, k, v, kk, a, S0):
    def step(S, inp):
        r_t, w_t, k_t, v_t, kk_t, a_t = inp
        sa = -jnp.einsum('bhvk,bhk->bhv', S, kk_t)
        S = (S * w_t[:, :, None, :] + sa[..., None] * (kk_t * a_t)[:, :, None, :]
             + v_t[..., None] * k_t[:, :, None, :])
        return S, jnp.einsum('bhvk,bhk->bhv', S, r_t)

    xs = tuple(jnp.moveaxis(t, 1, 0) for t in (r, decay, k, v, kk, a))
    S, ys = lax.scan(step, S0, xs)
    return jnp.moveaxis(ys, 0, 1), S

def rwkv7_time_mix(zx, S0, w0, w_decay_up, a0, w_iclr_up, w_rg_up, k_k, k_a, r_k, gn_g, gn_b):
    B, T, _ = zx.shape
    cuts = [D_RWKV, 2 * D_RWKV, 3 * D_RWKV, 3 * D_RWKV + DECAY_RANK, 3 * D_RWKV + DECAY_RANK + ICLR_RANK]
    r, kx, v, wd, ad, gd = jnp.split(zx, cuts, axis=-1)
    f32 = lambda t: t.astype(jnp.float32)
    heads = lambda t: t.reshape(B, T, N_HEADS_B, HEAD_DIM_B)
    hshape = (N_HEADS_B, HEAD_DIM_B)
    w_log = -jax.nn.softplus(-f32(w0 + jnp.tanh(wd) @ w_decay_up)) - 0.5
    decay = jnp.exp(-jnp.exp(w_log))
    a = heads(jax.nn.sigmoid(f32(a0 + ad @ w_iclr_up)))
    g = jax.nn.sigmoid(gd) @ w_rg_up
    kk = heads(f32(kx * k_k))
    kk = kk * lax.rsqrt(jnp.maximum(jnp.sum(kk * kk, axis=-1, keepdims=True), 1e-24))
    k_h = heads(f32(kx)) * (1.0 + (a - 1.0) * f32(k_a).reshape(hshape))
    r_h, v_h = heads(f32(r)), heads(f32(v))
    y, S = wkv7_scan(r_h, heads(decay), k_h, v_h, kk, a, f32(S0))
    mean = jnp.mean(y, axis=-1, keepdims=True)
    var = jnp.mean(jnp.square(y - mean), axis=-1, keepdims=True)
    y = (y - mean) * lax.rsqrt(var + GN_EPS) * f32(gn_g).reshape(hshape) + f32(gn_b).reshape(hshape)
    y = y + jnp.sum(r_h * k_h * f32(r_k), axis=-1, keepdims=True) * v_h
    return y.reshape(B, T, D_RWKV).astype(zx.dtype) * g, S

def layer(x, c, attn_fn, wkv0, shift0, w_ada, b_ada, g_norm, w_in, rel_bias, mu, w0, w_decay_up,
          a0, w_iclr_up, w_rg_up, k_k, k_a, r_k, gn_g, gn_b, w_out_attn, w_out_rwkv, w_out,
          w_ffn_in, w_ffn_out):
    B, T, _ = x.shape
    mod = jax.nn.silu(c) @ w_ada + b_ada
    sh1, sc1, gt1, sh2, sc2, gt2 = jnp.split(mod[:, None, :], 6, axis=-1)
    h = rmsnorm(x, g_norm[0]) * (1 + sc1) + sh1
    z = h @ w_in
    qkv = z[..., :3 * D_ATTN].reshape(B, T, 3, N_HEADS_A, HEAD_DIM_A)
    q, k, v = qkv[:, :, 0], qkv[:, :, 1], qkv[:, :, 2]
    zs = z[..., 3 * D_ATTN:3 * D_ATTN + SHIFT_COLS]
    gates = jax.nn.sigmoid(z[..., 3 * D_ATTN + SHIFT_COLS:])
    o_a = attn_fn(q, k, v, rel_bias).reshape(B, T, D_ATTN)
    prev = jnp.concatenate([shift0[:, None, :].astype(zs.dtype), zs[:, :-1]], axis=1)
    zx = zs + (prev - zs) * mu
    o_b, wkv1 = rwkv7_time_mix(zx, wkv0, w0, w_decay_up, a0, w_iclr_up, w_rg_up, k_k, k_a, r_k, gn_g, gn_b)
    merged = gates[..., :D_MODEL] * (o_a @ w_out_attn) + gates[..., D_MODEL:] * (o_b @ w_out_rwkv)
    x = x + gt1 * (merged @ w_out)
    h2 = rmsnorm(x, g_norm[1]) * (1 + sc2) + sh2
    u, gg = jnp.split(h2 @ w_ffn_in, 2, axis=-1)
    x = x + gt2 * ((jax.nn.silu(gg) * u) @ w_ffn_out)
    return x, k, v, wkv1.astype(x.dtype), zs[:, -1]

def setup_inputs(seed: int = 0) -> dict:
    key = jax.random.key(seed)
    ks = iter(jax.random.split(key, 40))
    nrm = lambda shape, s: jax.random.normal(next(ks), shape, jnp.float32) * s
    W = min(BAND_LEFT, PAST_LEN)
    return {
        'x_prompt': nrm((BATCH, SEQ, D_MODEL), 1.0),
        'x_sample': nrm((DEC_BATCH, DEC_SEQ, D_MODEL), 1.0),
        'cache_attn_k': nrm((DEPTH, DEC_BATCH, W, N_HEADS_A, HEAD_DIM_A), 1.0),
        'cache_attn_v': nrm((DEPTH, DEC_BATCH, W, N_HEADS_A, HEAD_DIM_A), 1.0),
        'state_wkv': nrm((DEPTH, DEC_BATCH, N_HEADS_B, HEAD_DIM_B, HEAD_DIM_B), 0.5),
        'state_shift': nrm((DEPTH, DEC_BATCH, SHIFT_COLS), 1.0),
        'c_prompt': nrm((BATCH, D_MODEL), 1.0),
        'c_sample': nrm((DEC_BATCH, D_MODEL), 1.0),
        'w_ada': nrm((DEPTH, D_MODEL, 6 * D_MODEL), 0.5 * D_MODEL ** -0.5),
        'b_ada': nrm((DEPTH, 6 * D_MODEL), 0.02),
        'g_norm': 1.0 + nrm((DEPTH, 2, D_MODEL), 0.05),
        'w_in': nrm((DEPTH, D_MODEL, PROJ_COLS), D_MODEL ** -0.5),
        'rel_bias': nrm((DEPTH, N_HEADS_A, N_REL), 0.5),
        'mu': jax.random.uniform(next(ks), (DEPTH, SHIFT_COLS), jnp.float32),
        'w0': nrm((DEPTH, D_RWKV), 0.5),
        'w_decay_up': nrm((DEPTH, DECAY_RANK, D_RWKV), 0.5 * DECAY_RANK ** -0.5),
        'a0': nrm((DEPTH, D_RWKV), 0.5),
        'w_iclr_up': nrm((DEPTH, ICLR_RANK, D_RWKV), 0.5 * ICLR_RANK ** -0.5),
        'w_rg_up': nrm((DEPTH, GATE_RANK, D_RWKV), GATE_RANK ** -0.5),
        'k_k': 0.85 + nrm((DEPTH, D_RWKV), 0.1),
        'k_a': 1.0 + nrm((DEPTH, D_RWKV), 0.1),
        'r_k': nrm((DEPTH, N_HEADS_B, HEAD_DIM_B), 0.1),
        'gn_g': 1.0 + nrm((DEPTH, D_RWKV), 0.05),
        'gn_b': nrm((DEPTH, D_RWKV), 0.02),
        'w_out_attn': nrm((DEPTH, D_ATTN, D_MODEL), D_ATTN ** -0.5),
        'w_out_rwkv': nrm((DEPTH, D_RWKV, D_MODEL), D_RWKV ** -0.5),
        'w_out': nrm((DEPTH, D_MODEL, D_MODEL), D_MODEL ** -0.5),
        'w_ffn_in': nrm((DEPTH, D_MODEL, 2 * D_FF), D_MODEL ** -0.5),
        'w_ffn_out': nrm((DEPTH, D_FF, D_MODEL), D_FF ** -0.5),
        'g_final': 1.0 + nrm((D_MODEL,), 0.05),
    }

def reference(x_prompt, x_sample, cache_attn_k, cache_attn_v, state_wkv, state_shift, c_prompt, c_sample,
              w_ada, b_ada, g_norm, w_in, rel_bias, mu, w0, w_decay_up, a0, w_iclr_up, w_rg_up, k_k, k_a,
              r_k, gn_g, gn_b, w_out_attn, w_out_rwkv, w_out, w_ffn_in, w_ffn_out, g_final):
    Bp, T, _ = x_prompt.shape
    n_keep = min(BAND_LEFT, T)
    zero_S = jnp.zeros((Bp, N_HEADS_B, HEAD_DIM_B, HEAD_DIM_B), jnp.float32)
    zero_shift = jnp.zeros((Bp, SHIFT_COLS), x_prompt.dtype)
    xp, xs = x_prompt, x_sample
    kp_l, vp_l, Sp_l, shp_l, ks_l, vs_l, Ss_l, shs_l = [], [], [], [], [], [], [], []
    for l in range(DEPTH):
        lw = (w_ada[l], b_ada[l], g_norm[l], w_in[l], rel_bias[l], mu[l], w0[l], w_decay_up[l], a0[l],
              w_iclr_up[l], w_rg_up[l], k_k[l], k_a[l], r_k[l], gn_g[l], gn_b[l], w_out_attn[l],
              w_out_rwkv[l], w_out[l], w_ffn_in[l], w_ffn_out[l])
        xp, k, v, S, sh = layer(xp, c_prompt, chunk_band_attention, zero_S, zero_shift, *lw)
        kp_l.append(k[:, T - n_keep:])
        vp_l.append(v[:, T - n_keep:])
        Sp_l.append(S)
        shp_l.append(sh)
        sample_attn = functools.partial(cached_band_attention, k_cache=cache_attn_k[l], v_cache=cache_attn_v[l])
        xs, k, v, S, sh = layer(xs, c_sample, sample_attn, state_wkv[l], state_shift[l], *lw)
        ks_l.append(k)
        vs_l.append(v)
        Ss_l.append(S)
        shs_l.append(sh)
    y_prompt = rmsnorm(xp, g_final)
    y_sample = rmsnorm(xs, g_final)
    new_k_prompt = jnp.stack(kp_l)
    new_v_prompt = jnp.stack(vp_l)
    new_wkv_prompt = jnp.stack(Sp_l)
    new_shift_prompt = jnp.stack(shp_l)
    new_k_sample = jnp.stack(ks_l)
    new_v_sample = jnp.stack(vs_l)
    new_wkv_sample = jnp.stack(Ss_l)
    new_shift_sample = jnp.stack(shs_l)
    return (y_prompt, y_sample, new_k_prompt, new_v_prompt, new_wkv_prompt, new_shift_prompt,
            new_k_sample, new_v_sample, new_wkv_sample, new_shift_sample)


_drawn_inputs = setup_inputs


def setup_inputs(seed=0):
    import zlib

    import numpy as np

    out = dict(_drawn_inputs(seed))
    spreads = {}
    factors = {'cache_attn_k': 5.523,
     'cache_attn_v': 4.749,
     'state_wkv': 2.713,
     'state_shift': 3.541,
     'rel_bias': 5.99,
     'gn_g': 8.0,
     'gn_b': 41.46}
    for name, (base, spread) in spreads.items():
        noise = np.random.default_rng([zlib.crc32(name.encode()), seed]).standard_normal(out[name].shape)
        drawn = base * np.exp(spread * noise) if base else spread * noise
        out[name] = __import__('jax').numpy.asarray(drawn.astype(out[name].dtype))
    for name, factor in factors.items():
        out[name] = (out[name] * factor).astype(out[name].dtype)
    return out
```

```python
from contextlib import ExitStack, contextmanager

import concourse.bass as bass
from concourse import mybir

F32 = mybir.dt.float32
F32R = mybir.dt.float32r
ACT = mybir.ActivationFunctionType
ALU = mybir.AluOpType
AX = mybir.AxisListType.X

P = 128
KAPPA = 0.6065306597126334
RMS_EPS, GN_EPS, KK_MIN, NEG = 1e-6, 64e-5, 1e-24, -1e30


class Chain:

    def __init__(self, eng, sem):
        self.eng, self.sem, self.base, self.n, self.total = eng, sem, 0, 0, 0

    def __call__(self, ins):
        self.n += 1
        ins.then_inc(self.sem, 1)
        self.eng.wait_ge(self.sem, self.base + self.n)

    @contextmanager
    def loop(self, trips, per):
        before = self.base + self.n
        with self.eng.Fori(0, trips) as it:
            self.base, self.n = it * per + before, 0
            yield it
            assert self.n == per, f"{self.n} chained, not {per}"
        self.base, self.n = before + trips * per, 0


def build(nc, x_prompt, x_sample, cache_k, cache_v, state_wkv, state_shift, c_prompt, c_sample, w_ada, b_ada,
          g_norm, w_in, rel_bias, mu, w0, w_decay_up, a0, w_iclr_up, w_rg_up, k_k, k_a, r_k, gn_g, gn_b,
          w_out_attn, w_out_rwkv, w_out, w_ffn_in, w_ffn_out, g_final,
          y_prompt, y_sample, nk_prompt, nv_prompt, nwkv_prompt, nshift_prompt, nk_sample, nv_sample,
          nwkv_sample, nshift_sample):
    T, D = x_prompt.shape[1:]
    TS = x_sample.shape[1]
    L = 64
    PAD = 4
    S0 = T + PAD
    W = S0 + TS
    H = W // 2
    KD = D // P
    NH, DH = 8, 64
    DA = NH * DH
    HP = DA // P
    SC = mu.shape[1]
    ZT = SC // P
    FF = w_ffn_out.shape[1]
    FT = FF // P
    TT = T // P
    NCH = T // L
    NR = rel_bias.shape[2]
    CLIP = NR - L
    EXT = 640
    EOFF = 3 * P - 1
    assert H % 2 == 0 and H <= 512 and T == 512 and D == 1024 and CLIP == P and cache_k.shape[2] == 512
    UC = 2048

    ctx = ExitStack()
    with ctx:
        def sb(name, shape, dt=F32, where=ctx):
            return where.enter_context(nc.sbuf_tensor(name, shape, dt))

        def sem(name):
            return ctx.enter_context(nc.semaphore(name))


        xT = sb("xT", [P, KD, W])
        cs, aa = xT[:, 0:HP], xT[:, HP:2 * HP]
        w_raw = sb("w_raw", [P, 2, UC])
        hh = sb("hh", [P, KD, W], F32R)
        hl = sb("hl", [P, KD, W], F32R)
        ident = sb("ident", [P, P])
        anti = sb("anti", [P, P])
        ones = sb("ones", [P, P])
        N1, N2 = 10 * KD, 2 * ZT + 7 * HP
        par = sb("par", [P, N1 + N2])
        sc2 = sb("sc2", [P, KD, 2])
        mod = sb("mod", [P, 6 * KD, 2])
        gsc = sb("gsc", [P, 2, KD, 2])
        stat = sb("stat", [P, 16])
        omka = sb("omka", [P, HP])

        def scope(shapes):
            with ExitStack() as s:
                return [sb(n, shape, dt, s) for n, shape, dt in shapes]

        KS = TT + 1
        qs, ks, vs, kc_raw, kcT, vcs, s_sb, pt_sb, otok, rsum = scope([
            ("qs", [P, W], F32), ("ks", [P, W], F32), ("vs", [P, KS, P], F32), ("kc_raw", [P, TT, P], F32),
            ("kcT", [P, T], F32), ("vcs", [P, TT, P], F32), ("s_sb", [P, 2, T + TS], F32),
            ("pt_sb", [P, 2, T + P], F32), ("otok", [P, KS, P], F32), ("rsum", [P, 2, 4], F32)])
        made = scope([("bl", [P, W], F32), ("kl", [P, W], F32), ("vst", [P, W], F32),
                      ("E2", [P, W], F32), ("kh", [P, W], F32)] +
                     [(f"{n}{q}", [P, c, P], F32) for q in range(2)
                      for n, c in (("ATs", 2), ("BDs", 4), ("CTs", 2), ("X", 2), ("XT", 2), ("Pb", 2), ("KC", 2),
                                   ("WU", 2), ("tk", 3))])
        bl, kl, vst, E2, kh = made[:5]
        ATs, BDs, CTs, X, XT, Pb, KC, WU, tk = [[made[5 + 9 * q + i] for q in range(2)] for i in range(9)]
        w_hi = sb("w_hi", [P, 2, UC], F32R)
        w_lo = sb("w_lo", [P, 2, UC], F32R)
        ah, al, ff_g, ff_a, gf_row = scope([("ah", [P, FT, W], F32R), ("al", [P, FT, W], F32R),
                                    ("ff_g", [P, W], F32), ("ff_a", [P, W], F32), ("gf_row", [P, D], F32)])
        y_sb, y_sq = scope([("y_sb", [P, 2, D], F32), ("y_sq", [P, D], F32)])
        mgh, sg1, sg2, mt = scope([("mgh", [P, KD, W], F32R), ("sg1", [P, 2, W], F32), ("sg2", [P, 2, W], F32),
                                   ("mt", [P, 2, W], F32)])
        zs = sb("zs", [P, ZT, W + 1])
        oaT = sb("oaT", [P, HP, W])
        (rows1, rows2, xtok, xtok_s, sq_a, rstd, tmp_a, rbx) = scope([
            ("rows1", [N1, P], F32), ("rows2", [N2, P], F32), ("xtok", [P, TT, D], F32), ("xtok_s", [TS, D], F32),
            ("sq_a", [P, 2, W], F32), ("rstd", [P, W], F32),
            ("tmp_a", [P, 2, W], F32), ("rbx", [NH, EXT + NR], F32)])
        (qkvT, vtok, ktok, bias, shst, shrow) = scope([
            ("qkvT", [P, 3 * HP, W], F32), ("vtok", [P, KS, DA], F32), ("ktok", [P, 2, DA], F32),
            ("bias", [P, NH, T], F32), ("shst", [P, 2, ZT], F32), ("shrow", [2 * ZT, P], F32)])
        obh, obl, oah, oal, mgl = scope([
            ("obh", [P, HP, W], F32R), ("obl", [P, HP, W], F32R), ("oah", [P, HP, W], F32R),
            ("oal", [P, HP, W], F32R), ("mgl", [P, KD, W], F32R)])
        (MT, NN, SS, kk, bones, strictU, inclU, nM0, nM0T, lmask, resetm, ind, indT, dg2, wup, wrg, E1,
         kt, rt, bh, ss8, stv) = scope([
             ("MT", [P, HP, NCH + 1, DH], F32), ("NN", [P, HP, NCH + 1, DH], F32),
             ("SS", [P, NCH + 2, HP, DH], F32), ("kk", [P, HP, W], F32),
             ("bones", [P, P], F32), ("strictU", [P, P], F32), ("inclU", [P, P], F32), ("nM0", [P, P], F32),
             ("nM0T", [P, P], F32), ("lmask", [P, 5, 2, P], F32), ("resetm", [P, W], F32), ("ind", [P, HP, NH], F32),
             ("indT", [NH, HP, P], F32), ("dg2", [P, DH], F32), ("wup", [P, DA], F32), ("wrg", [P, DA], F32),
             ("E1", [P, W + 1], F32), ("kt", [P, W], F32), ("rt", [P, W], F32),
             ("bh", [P, W], F32), ("ss8", [NH, W], F32), ("stv", [P, HP, DH], F32)])
        fin_sb = bh[:, 0:2 * HP * DH].rearrange("p (i a k) -> p i a k", i=2, a=HP)
        ps = ctx.enter_context(nc.psum_tensor("ps", [P, 8, 512], F32))

        def pair(q):
            return ps[:, 2 * q:2 * q + 2, 0:H]

        def halves(ap):
            return ap.rearrange("p (h c) -> p h c", h=2)

        x_spill = nc.dram_tensor("x_spill", [P, KD, W], F32, kind="Internal").ap()
        ext_d = nc.dram_tensor("ext_d", [NH, EXT], F32, kind="Internal").ap()

        CP, CS_, GN_, BADA = 0, KD, 2 * KD, 4 * KD
        MU = N1
        SSH = MU + ZT
        W0, A0, KKc, KAc, RKc, GG, GB = [SSH + ZT + HP * i for i in range(7)]
        SH1, SCL1, GT1, SH2, SCL2, GT2 = [KD * i for i in range(6)]

        rows_in, x_in, rb_in, ext_out, bias_in = [sem(n) for n in ("rows_in", "x_in", "rb_in", "ext_out", "bias_in")]
        raw_in = [sem(f"raw_in{s}") for s in range(2)]
        consts_made = sem("consts_made")
        past_wait = sem("past_wait")
        rw_consts = sem("rw_consts")
        act_c, dve_c, pool_c = sem("act_chain"), sem("dve_chain"), sem("pool_chain")
        tile_mm, pair_free = sem("tile_mm"), sem("pair_free")
        par_ready, sig_c, sc2_ready = sem("par_ready"), sem("sig_c"), sem("sc2_ready")
        ada_used, ada_mm, mod_ready = sem("ada_used"), sem("ada_mm"), sem("mod_ready")
        sq_done, ss_mm, var_ready, rstd_ready = sem("sq_done"), sem("ss_mm"), sem("var_ready"), sem("rstd_ready")
        h_f32, hh_done, h_done = sem("h_f32"), sem("hh_done"), sem("h_done")
        hi_done, lo_done, unit_mm = sem("hi_done"), sem("lo_done"), sem("unit_mm")
        spilled, x_back = sem("spilled"), sem("x_back")
        ktok_mm, vtok_mm, ktok_ev, vtok_ev, vtok_out, oah_done = [sem(n) for n in (
            "ktok_mm", "vtok_mm", "ktok_ev", "vtok_ev", "vtok_out", "oah_done")]
        ktok_out = [sem(f"ktok_out{q}") for q in range(2)]
        flip_mm, flip_ev = sem("flip_mm"), sem("flip_ev")
        ext_made, hp_free = sem("ext_made"), sem("hp_free")
        zs_ready, shift_st, shift_mm, shift_out = [sem(n) for n in ("zs_ready", "shift_st", "shift_mm", "shift_out")]
        kc_in, vc_in, kct_mm, kct_ev, staged = [sem(n) for n in ("kc_in", "vc_in", "kct_mm", "kct_ev", "staged")]
        s_mm, s_biased, p_done, pt_mm, pt_ev, o_mm, o_ev, ot_mm, ot_ev = [sem(n) for n in (
            "s_mm", "s_biased", "p_done", "pt_mm", "pt_ev", "o_mm", "o_ev", "ot_mm", "ot_ev")]
        up_in, zx_done, td_done, up_mm, up_ev, kkr_done, kksq, kk_mm, kkv, rkk, kkb_mm, kk_ready = [sem(n) for n in (
            "up_in", "zx_done", "td_done", "up_mm", "up_ev", "kkr_done", "kksq", "kk_mm", "kkv", "rkk",
            "kkb_mm", "kk_ready")]
        exps, vst_done, ew_done, rk_done, bon_mm = [sem(n) for n in (
            "exps", "vst_done", "ew_done", "rk_done", "bon_mm")]
        sc_mm, at_ev, tk_ev, masked, cv_mm, cv_ev, x0_done = [sem(n) for n in (
            "sc_mm", "at_ev", "tk_ev", "masked", "cv_mm", "cv_ev", "x0_done")]
        lev_p_mm = [sem(f"lev_p_mm{q}") for q in range(2)]
        lev_p = [sem(f"lev_p{q}") for q in range(2)]
        lev_x_mm = [sem(f"lev_x_mm{q}") for q in range(2)]
        lev_x = [sem(f"lev_x{q}") for q in range(2)]
        wu_mm, wu_ev, gm_mm, gm_dve, gm_act = [sem(n) for n in ("wu_mm", "wu_ev", "gm_mm", "gm_dve", "gm_act")]
        st_in, st_mm, st_ev, chain_mm, chain_ev, fin_mm, fin_ev, wkv_out = [sem(n) for n in (
            "st_in", "st_mm", "st_ev", "chain_mm", "chain_ev", "fin_mm", "fin_ev", "wkv_out")]
        y_mm, y_done, mean_mm, yc_done, ysq, var_mm, var8, rs8, rsb_mm, gate_mm, ob_f32, obh_done, ob_done = [
            sem(n) for n in ("y_mm", "y_done", "mean_mm", "yc_done", "ysq", "var_mm", "var8", "rs8", "rsb_mm",
                             "gate_mm", "ob_f32", "obh_done", "ob_done")]
        sig1, mg_f32, mgh_done, mg_done, x1_done, ffg, act_f32, ah_done, act_done = [sem(n) for n in (
            "sig1", "mg_f32", "mgh_done", "mg_done", "x1_done", "ffg", "act_f32", "ah_done", "act_done")]
        gf_in, yt_mm, ysq_done, yv, yr, yt_done = [sem(n) for n in (
            "gf_in", "yt_mm", "ysq_done", "yv", "yr", "yt_done")]
        y_out = [sem(f"y_out{q}") for q in range(2)]

        block = ctx.enter_context(nc.Block())

        UW = 256
        NQKV, NZS = 3 * DA // UW, SC // UW
        NMG, NWO, NUP, NDN = 3 * (D // UW), D // UW, FT, 2 * KD
        NADA1, NADA2 = 2 * D // UW, 4 * D // UW
        U_ZS = NQKV
        U_MG = U_ZS + NZS
        U_WO = U_MG + NMG
        U_UP = U_WO + NWO
        U_DN = U_UP + NUP
        KDN = FT // 2
        R_LATE = NADA1 + NADA2
        assert NADA1 % 2 == 0 and NADA2 % 2 == 0 and NQKV % 2 == 0 and NZS % 2 == 1
        T_QKV = 2 + TT
        T_ZS = T_QKV + 2 * NQKV
        T_MG = T_ZS + 2 * NZS
        T_WO = T_MG + 8 * (D // UW)
        T_UP = T_WO + 2 * NWO
        T_DN = T_UP + 2 * NUP
        T_Y = T_DN + KD
        M_QKV = T_QKV
        M_MG = M_QKV + U_MG
        M_WO = M_MG + 5 * (D // UW)
        M_UP = M_WO + NWO
        TILES = [(t * P, P) for t in range(TT)] + [(S0, TS)]

        PAIRS = [(0, 1), (2, 3), (4,)]

        def n_levels(R):
            return 5 if R == P else 4

        def lev_at(t, lev):
            return sum(n_levels(TILES[u][1]) for u in range(t % 2, t, 2)) + lev
        LEVS = [lev_at(4, n_levels(TS)), lev_at(3, n_levels(P))]

        def bank(q, i):
            return ps[:, 4 * q + i, :].rearrange("p (a c) -> p a c", a=4)

        def two_by_two(eng, first, n, body):
            end = first + n - n % 2
            if end > first:
                with eng.Fori(0, n // 2) as twice:
                    body(twice * 2 + first, first % 2)
                    body(twice * 2 + (first + 1), (first + 1) % 2)
            if n % 2:
                body(end, end % 2)

        def wait_alone(eng, sem_, value):
            eng.wait_ge(sem_, value)
            eng.sem_inc(past_wait, 1)

        @block.sync
        def _(sp):
            w8 = lambda w: w[0].rearrange("(k p) c -> p k c", p=P)

            def slot(s, k0, k1, kn=8):
                return w_raw[:, s, :].rearrange("p (k c) -> p k c", k=kn)[:, k0:k1, :]

            def columns(w, col, s):
                sp.dma_start(slot(s, 0, 4), w8(w)[:, 0:4, bass.ds(col, UW)]).then_inc(raw_in[s], 16)
                sp.dma_start(slot(s, 4, 8), w8(w)[:, 4:8, bass.ds(col, UW)]).then_inc(raw_in[s], 16)

            for i in range(2):
                columns(w_ada, i * UW, i)

            def ada(i, s):
                sp.wait_ge(ada_used, i - 1)
                columns(w_ada, i * UW, s)
            two_by_two(sp, 2, NADA1 - 2, ada)
            sp.wait_ge(ada_used, NADA1)
            for i in range(2):
                columns(w_in, i * UW, i)

            def project(i, s):
                sp.wait_ge(lo_done, i - 1)
                columns(w_in, i * UW, s)
            two_by_two(sp, 2, NQKV + NZS - 2, project)
            sp.wait_ge(h_done, KD)
            sp.dma_start(x_spill, xT[:, :, :]).then_inc(spilled, 16)
            sp.wait_ge(lo_done, NQKV + NZS)

            def ada_late(i, s):
                sp.wait_ge(ada_used, i - 1)
                columns(w_ada, i * UW, 1 - s)
            for i in range(2):
                columns(w_ada, (NADA1 + i) * UW, 1 - i)
            two_by_two(sp, NADA1 + 2, NADA2 - 2, ada_late)
            sp.wait_ge(ada_used, NADA1 + NADA2)

            sp.wait_ge(lo_done, U_MG)
            with sp.Fori(0, D // UW // 2) as g2:
                for j in range(6):
                    s = (U_MG + j) % 2
                    wait_alone(sp, lo_done, g2 * 6 + (U_MG + j - 1))
                    col = g2 * (2 * UW) + (j // 3) * UW
                    if j % 3 < 2:
                        columns(w_in, col + (3 * DA + SC + (j % 3) * D), s)
                    else:
                        for b, w in enumerate((w_out_attn, w_out_rwkv)):
                            sp.dma_start(slot(s, 4 * b, 4 * b + 4),
                                         w8(w)[:, :, bass.ds(col, UW)]).then_inc(raw_in[s], 16)

            def outw(i, s):
                sp.wait_ge(lo_done, i - 1)
                columns(w_out, i * UW - U_WO * UW, s)
            two_by_two(sp, U_WO, NWO, outw)
            sp.wait_ge(ob_done, HP)
            sp.dma_start(xT[:, :, :], x_spill).then_inc(x_back, 16)
            sp.wait_ge(wkv_out, 32)
            sp.dma_start(gf_row[:, :], g_final.unsqueeze(0).to_broadcast([P, D])).then_inc(gf_in, 16)

            def up(i, s):
                sp.wait_ge(lo_done, i - 1)
                for b in range(2):
                    sp.dma_start(slot(s, 0, 8)[:, :, b * P:b * P + P],
                                 w8(w_ffn_in)[:, :, bass.ds(i * P + (b * FF - U_UP * P), P)]).then_inc(raw_in[s], 16)
            two_by_two(sp, U_UP, NUP, up)
            wd = w_ffn_out[0].rearrange("(k p) c -> p k c", p=P)
            dn = lambda s, a, b: w_raw[:, s, 0:KDN * P].rearrange("p (k c) -> p k c", k=KDN)[:, a:b, :]
            with sp.Fori(0, KD) as m:
                for j in range(2):
                    s = (U_DN + j) % 2
                    sp.wait_ge(lo_done, m * 2 + (U_DN + j - 1))
                    for a, b in ((0, KDN // 2), (KDN // 2, KDN)):
                        sp.dma_start(dn(s, a, b), wd[:, j * KDN + a:j * KDN + b, bass.ds(m * P, P)])\
                          .then_inc(raw_in[s], 16)
            for t, (_, rows) in enumerate(TILES):
                sp.wait_ge(yt_done, t + 1)
                dst = y_prompt[0, t * P:(t + 1) * P, :] if t < TT else y_sample[0]
                sp.dma_start(dst, y_sb[0:rows, t % 2, :]).then_inc(y_out[t % 2], 16)
            for q in range(2):
                sp.wait_ge(y_out[q], 16 * ((len(TILES) + 1 - q) // 2))
            sp.wait_ge(ktok_out[0], 16 * 3)
            sp.wait_ge(ktok_out[1], 16 * 2)
            sp.wait_ge(vtok_out, 16 * len(TILES))
            sp.wait_ge(shift_out, 32)
            sp.wait_ge(wkv_out, 32)

        @block.gpsimd
        def _(pool):
            link = Chain(pool, pool_c)

            def select(ap, pattern, base, cm, op, fill):
                return pool.affine_select(out=ap, in_=ap, pattern=pattern, base=base, channel_multiplier=cm,
                                          compare_op=op, fill=fill)

            link(pool.memset(ident[:, :], 0.0))
            link(pool.memset(anti[:, :], 0.0))
            pool.memset(ones[:, :], 1.0).then_inc(consts_made, 1)
            select(ident[:, :], [[-1, P]], 0, 1, ALU.not_equal, 1.0).then_inc(consts_made, 1)
            select(anti[:, :], [[1, P]], 1 - P, 1, ALU.not_equal, 1.0).then_inc(consts_made, 1)

            def low(i, s, cols=UC):
                pool.wait_ge(hi_done, i + 1)
                if not isinstance(i, int) or i >= 2:
                    pool.wait_ge(unit_mm, i - 1)
                pool.tensor_tensor(w_lo[:, s, 0:cols], w_raw[:, s, 0:cols], w_hi[:, s, 0:cols].bitcast(F32),
                                   ALU.subtract).then_inc(lo_done, 1)
            low(0, 0)
            low(1, 1)
            two_by_two(pool, 2, NQKV + NZS - 2, low)
            pool.wait_ge(up_in, 48)
            link(pool.memset(bones[:, :], 0.0))
            link(pool.memset(bones[0:DH, 0:DH], 1.0))
            link(pool.memset(bones[DH:P, DH:P], 1.0))
            link(pool.tensor_copy(strictU[:, :], bones[:, :]))
            link(pool.tensor_copy(inclU[:, :], bones[:, :]))
            link(select(strictU[:, :], [[1, P]], 0, -1, ALU.is_gt, 0.0))
            link(select(inclU[:, :], [[1, P]], 0, -1, ALU.is_ge, 0.0))
            link(pool.memset(nM0[:, :], 0.0))
            link(pool.memset(nM0T[:, :], 0.0))
            two = lambda m: m[:, :].rearrange("p (b two) -> p b two", two=2)
            link(select(two(nM0)[:, :, 0], [[-2, P // 2]], -1, 1, ALU.not_equal, -1.0))
            link(select(two(nM0T)[:, :, 1], [[-2, P // 2]], 0, 1, ALU.not_equal, -1.0))
            link(pool.memset(lmask[:, :, :, :], 0.0))
            for lev in range(5):
                s = 2 << lev
                for u in range(2):
                    v = lmask[:, lev, u, :].rearrange("p (b h s) -> p b h s", h=2, s=s)[:, :, 0, :]
                    nb = P // (2 * s)
                    link(pool.memset(v, 1.0))
                    link(select(v, [[-2 * s, nb], [0, s]], -s, 1, ALU.is_ge, 0.0))
                    link(select(v, [[2 * s, nb], [0, s]], 2 * s - 1, -1, ALU.is_ge, 0.0))
            link(pool.memset(resetm[:, :], 1.0))
            link(pool.memset(resetm[:, 0:T:L], 0.0))
            link(pool.memset(resetm[:, T:S0 + 1], 0.0))
            link(pool.memset(ind[:, :, :], 0.0))
            for hp in range(HP):
                for e in range(2):
                    link(pool.memset(ind[e * DH:e * DH + DH, hp, 2 * hp + e:2 * hp + e + 1], 1.0))
            link(pool.memset(indT[:, :, :], 0.0))
            link(select(indT[:, :, :].rearrange("h a (e d) -> h (a e) d", e=2), [[-1, NH], [0, DH]], 0, 1,
                        ALU.not_equal, 1.0))
            link(pool.memset(dg2[:, :], 0.0))
            link(select(dg2[:, :], [[-1, DH]], 0, 1, ALU.not_equal, 1.0))
            select(dg2[:, :], [[-1, DH]], -DH, 1, ALU.not_equal, 1.0).then_inc(rw_consts, 1)
            two_by_two(pool, U_MG, NMG + NWO + NUP, low)
            two_by_two(pool, U_DN, NDN, lambda i, s: low(i, s, KDN * P))

        @block.scalar
        def _(act):
            link = Chain(act, act_c)
            rows = lambda ap: ap.rearrange("(t p) -> t p", p=P)
            at = 0
            for v in (c_prompt[0], c_sample[0], g_norm[0, 0], g_norm[0, 1], b_ada[0]):
                n = v.shape[0] // P
                act.dma_start(rows1[at:at + n, :], rows(v)).then_inc(rows_in, 16)
                at += n
            at = 0
            rk_flat = r_k[0].rearrange("h d -> (h d)")
            for v in (mu[0], state_shift[0, 0], w0[0], a0[0], k_k[0], k_a[0], rk_flat, gn_g[0], gn_b[0]):
                n = v.shape[0] // P
                act.dma_start(rows2[at:at + n, :], rows(v)).then_inc(rows_in, 16)
                at += n
            act.dma_start(xtok[:, :, :], x_prompt[0].rearrange("(t p) d -> p t d", p=P)).then_inc(x_in, 16)
            act.dma_start(xtok_s[:, :], x_sample[0]).then_inc(x_in, 16)
            act.dma_start(rbx[:, EXT:EXT + NR], rel_bias[0]).then_inc(rb_in, 16)

            act.wait_ge(par_ready, 1)
            act.activation(stat[:, :], par[:, 0:2 * KD], ACT.Sigmoid).then_inc(sig_c, 1)
            act.wait_ge(ext_made, 1)
            act.dma_start(ext_d, rbx[:, 0:EXT]).then_inc(ext_out, 16)

            def norm(first):
                for k in range(KD):
                    if k >= 2:
                        act.wait_ge(ss_mm, first * KD + k - 1)
                    act.activation(sq_a[:, k % 2, :], xT[:, k, :], ACT.Square).then_inc(sq_done, 1)
                act.wait_ge(var_ready, first + 1)
                act.activation(rstd[:, :], rstd[:, :], ACT.Sqrt).then_inc(rstd_ready, 1)
                for k in range(KD):
                    act.wait_ge(h_f32, first * KD + k + 1)
                    act.activation(hh[:, k, :], tmp_a[:, k % 2, :], ACT.Copy).then_inc(hh_done, 1)

            act.wait_ge(pair_free, T_QKV - 1)
            norm(0)
            act.wait_ge(ext_out, 16)
            act.dma_start(bias[:, :, :], bass.AP(tensor=ext_d.tensor, offset=0, ap=[[1, P], [EXT, NH], [1, T]]))\
               .then_inc(bias_in, 16)

            def high(i, s, ahead, cols=UC):
                act.wait_ge(raw_in[s], (i + ahead) * 16 + (32 - 16 * s))
                if not isinstance(i, int) or i >= 2:
                    act.wait_ge(unit_mm, i - 1)
                act.activation(w_hi[:, s, 0:cols], w_raw[:, s, 0:cols], ACT.Copy).then_inc(hi_done, 1)

            def evacuate(q, dst, done, count, func=ACT.Copy):
                act.wait_ge(done, count)
                act.activation(halves(dst), pair(q), func).then_inc(pair_free, 1)

            high(0, 0, NADA1)

            def qkv_unit(i, s):
                high(i + 1, 1 - s, NADA1)
                evacuate(0, qkvT[:, i * 2, :], tile_mm, i + (M_QKV + 1))
                evacuate(1, qkvT[:, i * 2 + 1, :], unit_mm, i + 1)
            for i in range(2):
                qkv_unit(i, i)
            two_by_two(act, 2, NQKV - 2, qkv_unit)

            def zs_unit(i, s, more=True):
                if more:
                    high(i + 1, 1 - s, NADA1)
                evacuate(0, zs[:, i * 2 - 2 * U_ZS, 1:W + 1], tile_mm, i + (M_QKV + 1))
                evacuate(1, zs[:, i * 2 + (1 - 2 * U_ZS), 1:W + 1], unit_mm, i + 1)
            two_by_two(act, U_ZS, NZS - 1, zs_unit)
            zs_unit(U_MG - 1, (U_MG - 1) % 2, False)
            for t, (c0, rows_) in enumerate(TILES):
                act.wait_ge(ktok_mm, t + 1)
                if t >= 2:
                    act.wait_ge(ktok_out[t % 2], 16 * (t // 2))
                act.activation(ktok[0:rows_, t % 2, :], ps[0:rows_, t % 2, :], ACT.Copy).then_inc(ktok_ev, 1)
                flat = lambda o: o[0, 0].rearrange("t h e -> t (h e)")
                k_o = flat(nk_prompt)[c0:c0 + P, :] if t < TT else flat(nk_sample)
                v_o = flat(nv_prompt)[c0:c0 + P, :] if t < TT else flat(nv_sample)
                act.wait_ge(ktok_ev, t + 1)
                act.dma_start(k_o, ktok[0:rows_, t % 2, :]).then_inc(ktok_out[t % 2], 16)
                act.wait_ge(vtok_ev, t + 1)
                act.dma_start(v_o, vtok[0:rows_, t, :]).then_inc(vtok_out, 16)
            act.wait_ge(shift_mm, 1)
            act.activation(shrow[:, :], ps[0:2 * ZT, 6, 0:P], ACT.Copy).then_inc(shift_st, 1)
            act.wait_ge(shift_st, 1)
            rowsof = lambda o: o[0, 0].rearrange("(t p) -> t p", p=P)
            act.dma_start(rowsof(nshift_prompt), shrow[0:ZT, :]).then_inc(shift_out, 16)
            act.dma_start(rowsof(nshift_sample), shrow[ZT:2 * ZT, :]).then_inc(shift_out, 16)

            act.wait_ge(unit_mm, U_MG)
            kcv = lambda c: c[0, 0].rearrange("(t p) h e -> p t (h e)", p=P)
            NJ = 2 * len(TILES)
            with link.loop(HP, 1) as hp:
                act.dma_start(kc_raw[:, :, :], kcv(cache_k)[:, :, bass.ds(hp * P, P)]).then_inc(kc_in, 16)
                act.dma_start(vcs[:, :, :], kcv(cache_v)[:, :, bass.ds(hp * P, P)]).then_inc(vc_in, 16)
                act.activation(qs[:, :], qkvT[:, hp, :], ACT.Copy, scale=DH ** -0.5).then_inc(staged, 1)
                act.activation(ks[:, :], qkvT[:, hp + HP, :], ACT.Copy).then_inc(staged, 1)
                act.activation(vs[:, 0:TT, :], vtok[:, 0:TT, bass.ds(hp * P, P)], ACT.Copy).then_inc(staged, 1)
                act.activation(vs[0:TS, TT, :], vtok[0:TS, TT, bass.ds(hp * P, P)], ACT.Copy).then_inc(staged, 1)

                def pt_out(j):
                    t, rows_ = j // 2, TILES[j // 2][1]
                    act.wait_ge(pt_mm, hp * NJ + (j + 1))
                    n = (t + 1) * P if t < TT else TT * TS
                    act.activation(pt_sb[:, j % 2, 0:n], ps[:, 2 + j % 2, 0:n], ACT.Copy).then_inc(pt_ev, 1)
                    if t == TT:
                        act.activation(pt_sb[0:TS, j % 2, n:n + TS], ps[0:TS, 2 + j % 2, n:n + TS],
                                       ACT.Copy).then_inc(pt_ev, 1)
                for j in range(NJ + 1):
                    if j < NJ:
                        t, rows_ = j // 2, TILES[j // 2][1]
                        n = (t + 1) * P if t < TT else T + TS
                        act.wait_ge(s_biased, hp * NJ + (j + 1))
                        v = s_sb[0:rows_, j % 2, 0:n]
                        act.activation(v, v, ACT.Exp, bias=rsum[0:rows_, j % 2, 1:2],
                                       accum_out=rsum[0:rows_, j % 2, 0:1]).then_inc(p_done, 1)
                    if j == 5:
                        act.wait_ge(kct_mm, hp + 1)
                        act.activation(kcT[:, :], ps[:, 7, :], ACT.Copy).then_inc(kct_ev, 1)
                    if j:
                        pt_out(j - 1)
                act.wait_ge(ot_mm, hp + 1)
                link(act.activation(oaT[:, hp, 0:T], ps[:, 6, :], ACT.Copy))
                act.activation(oaT[:, hp, S0:W], ps[:, 7, 0:TS], ACT.Copy).then_inc(ot_ev, 1)

            act.wait_ge(ktok_out[0], 16 * 3)
            act.wait_ge(ktok_out[1], 16 * 2)
            act.wait_ge(vtok_out, 16 * len(TILES))
            act.wait_ge(shift_out, 32)
            act.wait_ge(ot_ev, HP)
            act.dma_start(wup[0:DH, :], w_decay_up[0]).then_inc(up_in, 16)
            act.dma_start(wup[DH:P, :], w_iclr_up[0]).then_inc(up_in, 16)
            act.dma_start(wrg[:, :], w_rg_up[0]).then_inc(up_in, 16)
            act.dma_start(stv[:, :, :], state_wkv[0, 0].rearrange("(a e) v k -> (e v) a k", e=2)).then_inc(st_in, 16)
            act.wait_ge(zx_done, 1)
            act.activation(zs[0:DH, ZT - 2, 1:W + 1], zs[0:DH, ZT - 2, 1:W + 1], ACT.Tanh).then_inc(td_done, 1)
            act.wait_ge(zx_done, 2)
            act.activation(zs[:, ZT - 1, 1:W + 1], zs[:, ZT - 1, 1:W + 1], ACT.Sigmoid).then_inc(td_done, 1)
            act.wait_ge(spilled, 16)
            for m in range(HP):
                for j, (dst, b) in enumerate(((cs, W0), (aa, A0))):
                    n = 2 * m + j
                    act.wait_ge(up_mm, n + 1)
                    act.activation(halves(dst[:, m, :]), pair(n % 4), ACT.Sigmoid,
                                   bias=par[:, b + m:b + m + 1]).then_inc(up_ev, 1)
            for m in range(HP):
                act.wait_ge(kkr_done, m + 1)
                if m >= 2:
                    act.wait_ge(kk_mm, m - 1)
                act.activation((kt, rt)[m % 2][:, :], kk[:, m, :], ACT.Square).then_inc(kksq, 1)
            act.wait_ge(kkv, 1)
            act.activation(ss8[:, :], ss8[:, :], ACT.Sqrt).then_inc(rkk, 1)

            with link.loop(HP, 2 * KS + TT) as hp:
                act.wait_ge(hp_free, hp + 1)
                act.activation(E1[:, 1:W + 1], cs[:, hp, :], ACT.Exp, scale=-KAPPA).then_inc(exps, 1)
                act.activation(E2[:, :], cs[:, hp, :], ACT.Exp, scale=KAPPA).then_inc(exps, 1)
                act.activation(vst[:, :], zs[:, hp + 2 * HP, 1:W + 1], ACT.Copy).then_inc(exps, 1)

                def a_scores(t, q, R):
                    act.wait_ge(sc_mm, hp * KS + (t + 1))
                    act.activation(ATs[q][0:R, :, 0:R], ps[0:R, 4 * q:4 * q + 2, 0:R], ACT.Copy).then_inc(at_ev, 1)
                    link(act.activation(KC[q][0:R, :, 0:DH],
                                        bank(q, 0)[0:R, 1, :].rearrange("p (e c) -> p e c", e=2), ACT.Copy))
                    act.activation(tk[q][0:R, :, :], bank(q, 1)[0:R, 1:4, :], ACT.Copy).then_inc(tk_ev, 1)

                def a_cv(t, q, R):
                    act.wait_ge(cv_mm, hp * KS + (t + 1))
                    act.activation(KC[q][0:R, :, DH:P], bank(q, 0)[0:R, 0, :].rearrange("p (e c) -> p e c", e=2),
                                   ACT.Copy).then_inc(cv_ev, 1)

                def a_wu(t, q, R):
                    act.wait_ge(wu_mm, hp * KS + (t + 1))
                    act.activation(WU[q][0:R, :, :], bank(q, 1)[0:R, 0:2, :], ACT.Copy, scale=-1.0).then_inc(wu_ev, 1)

                def a_out(t, q, R):
                    c0 = TILES[t][0]
                    wait_alone(act, gm_mm, hp * KS + (t + 1))
                    link(act.activation(zs[:, hp + 2 * HP, 1 + c0:1 + c0 + R], bank(q, 0)[:, 0, 0:R], ACT.Copy))
                    nch = 2 if t < TT else 1
                    if nch == 2:
                        link(act.activation(NN[:, hp, 2 * t + 1, :], bank(q, 0)[:, 1, 0:DH], ACT.Copy))
                    act.activation(NN[:, hp, 2 * t, :], bank(q, 1)[:, 0, 0:DH], ACT.Copy).then_inc(gm_act, 1)
                for tiles in PAIRS:
                    for stage in (a_scores, a_cv, a_wu, a_out):
                        for t in tiles:
                            stage(t, t % 2, TILES[t][1])

            act.wait_ge(fin_ev, 2)
            wk = lambda o: o[0, 0].rearrange("(a e) v k -> (e v) a k", e=2)
            act.dma_start(wk(nwkv_prompt), fin_sb[:, 0, :, :]).then_inc(wkv_out, 16)
            act.dma_start(wk(nwkv_sample), fin_sb[:, 1, :, :]).then_inc(wkv_out, 16)
            for m in range(HP):
                act.wait_ge(yc_done, m + 1)
                if m >= 2:
                    act.wait_ge(var_mm, m - 1)
                act.activation((kt, rt)[m % 2][:, :], zs[:, 2 * HP + m, 1:W + 1], ACT.Square).then_inc(ysq, 1)
            act.wait_ge(var8, 1)
            act.activation(ss8[:, :], ss8[:, :], ACT.Sqrt).then_inc(rs8, 1)
            act.wait_ge(ob_f32, 1)
            high(U_MG, U_MG % 2, R_LATE)
            act.activation(oah[:, :, :], oaT[:, :, :], ACT.Copy).then_inc(oah_done, 1)
            for m in range(HP):
                act.wait_ge(ob_f32, m + 1)
                act.activation(obh[:, m, :], (kt, rt)[m % 2][:, :], ACT.Copy).then_inc(obh_done, 1)

            with act.Fori(0, D // UW // 2) as g2:
                for j in range(6):
                    g, w = j // 3, j % 3
                    high(g2 * 6 + (U_MG + j + 1), (U_MG + j + 1) % 2, R_LATE)
                    if w < 2:
                        evacuate(0, (sg1, sg2)[w][:, 0, :], tile_mm, g2 * 10 + (M_MG + 5 * g + w + 1), ACT.Sigmoid)
                        evacuate(1, (sg1, sg2)[w][:, 1, :], unit_mm, g2 * 6 + (U_MG + j + 1), ACT.Sigmoid)
                    else:
                        for m in range(2):
                            act.wait_ge(mg_f32, g2 * 4 + (2 * g + m + 1))
                            act.activation(mgh[:, g2 * 4 + (2 * g + m), :], mt[:, 0, :], ACT.Copy).then_inc(mgh_done, 1)
            two_by_two(act, U_WO, NWO, lambda i, s: high(i + 1, 1 - s, R_LATE))
            act.wait_ge(pair_free, T_UP - 1)
            norm(1)

            def up(i, s, cols=UC):
                high(i + 1, 1 - s, R_LATE, cols)
                n = i * 2 + (T_UP - 2 * U_UP)
                act.wait_ge(pair_free, n - 1)
                evacuate(0, ff_g[:, :], tile_mm, i + (M_UP - U_UP + 1), ACT.Silu)
                act.wait_ge(pair_free, n + 1)
                act.activation(ah[:, i - U_UP, :], ff_a[:, :], ACT.Copy).then_inc(ah_done, 1)
            two_by_two(act, U_UP, NUP - 2, up)
            up(U_DN - 2, (U_DN - 2) % 2)
            up(U_DN - 1, (U_DN - 1) % 2, KDN * P)
            down = lambda i, s: high(i + 1, 1 - s, R_LATE, KDN * P)
            two_by_two(act, U_DN, NDN - 2, down)
            down(U_DN + NDN - 2, (U_DN + NDN - 2) % 2)

            for t, (_, rows_) in enumerate(TILES):
                act.wait_ge(yt_mm, t + 1)
                if t:
                    act.wait_ge(ysq_done, t)
                act.activation(y_sq[0:rows_, :].rearrange("p (b c) -> p b c", b=2), ps[0:rows_, 2 * (t % 2):2 * (t % 2) + 2, :],
                               ACT.Square, accum_out=stat[0:rows_, t:t + 1]).then_inc(ysq_done, 1)
                act.wait_ge(yv, t + 1)
                act.activation(stat[0:rows_, t:t + 1], stat[0:rows_, t:t + 1], ACT.Sqrt).then_inc(yr, 1)

        @block.vector
        def _(dve):
            link = Chain(dve, dve_c)
            tt, sts, stt = dve.tensor_tensor, dve.tensor_scalar, dve.scalar_tensor_tensor
            p1 = lambda c: par[:, c:c + 1]

            dve.wait_ge(tile_mm, 1)
            link(dve.tensor_copy(par[:, 0:N1], ps[:, 0, 0:N1]))
            dve.tensor_copy(par[:, N1:N1 + N2], ps[:, 0, P:P + N2]).then_inc(par_ready, 1)
            link(dve.memset(xT[:, :, T:S0], 0.0))
            dve.wait_ge(sig_c, 1)
            tt(sc2[:, :, :], par[:, 0:2 * KD].rearrange("p (s k) -> p k s", s=2),
               stat[:, :].rearrange("p (s k) -> p k s", s=2), ALU.mult).then_inc(sc2_ready, 1)
            for t, (c0, rows_) in enumerate(TILES):
                q = (t + 1) % 2
                dve.wait_ge(tile_mm, t + 2)
                src = ps[:, 2 * q:2 * q + 2, :].rearrange("p b (k c) -> p (b k) c", k=4)[:, :, 0:rows_]
                dve.tensor_copy(xT[:, :, c0:c0 + rows_], src).then_inc(pair_free, 1)
            dve.wait_ge(rb_in, 16)
            link(dve.tensor_copy(rbx[:, 0:EOFF], rbx[:, EXT:EXT + 1].to_broadcast([NH, EOFF])))
            link(dve.tensor_copy(rbx[:, EOFF:EOFF + NR], rbx[:, EXT:EXT + NR]))
            dve.tensor_copy(rbx[:, EOFF + NR:EXT], rbx[:, EXT + NR - 1:EXT + NR].to_broadcast([NH, EXT - EOFF - NR]))\
               .then_inc(ext_made, 1)

            def norm(i, sh, scl):
                dve.wait_ge(ss_mm, (i + 1) * KD)
                link(sts(halves(rstd[:, :]), pair(2), 1.0 / D, RMS_EPS, ALU.mult, ALU.add))
                dve.reciprocal(rstd[:, :], rstd[:, :]).then_inc(var_ready, 1)
                if i == 0:
                    dve.wait_ge(ada_used, NADA1)
                    link(tt(mod[:, 0:2 * KD, :], ps[:, 7, 0:4 * KD].rearrange("p (m s) -> p m s", s=2),
                            par[:, BADA:BADA + 2 * KD].unsqueeze(2).to_broadcast([P, 2 * KD, 2]), ALU.add))
                    scales(0)
                dve.wait_ge(rstd_ready, i + 1)
                for k in range(KD + 1):
                    if k < KD:
                        if k >= 2:
                            dve.wait_ge(h_done, i * KD + k - 1)
                        a = tmp_a[:, k % 2, :]
                        link(tt(a, xT[:, k, :], rstd[:, :], ALU.mult))
                        link(sts(a[:, 0:S0], a[:, 0:S0], gsc[:, i, k, 0:1], mod[:, sh + k, 0:1], ALU.mult, ALU.add))
                        sts(a[:, S0:W], a[:, S0:W], gsc[:, i, k, 1:2], mod[:, sh + k, 1:2],
                            ALU.mult, ALU.add).then_inc(h_f32, 1)
                    if k:
                        dve.wait_ge(hh_done, i * KD + k)
                        tt(hl[:, k - 1, :], tmp_a[:, (k - 1) % 2, :], hh[:, k - 1, :].bitcast(F32),
                           ALU.subtract).then_inc(h_done, 1)

            def scales(i):
                scl = (SCL1, SCL2)[i]
                link(stt(gsc[:, i, :, :], mod[:, scl:scl + KD, :], 1.0,
                         par[:, GN_ + i * KD:GN_ + (i + 1) * KD].unsqueeze(2).to_broadcast([P, KD, 2]),
                         ALU.add, ALU.mult))
            norm(0, SH1, SCL1)

            for t, (_, rows_) in enumerate(TILES):
                dve.wait_ge(vtok_mm, t + 1)
                dve.tensor_copy(vtok[0:rows_, t, :], ps[0:rows_, 2 + t % 2, :]).then_inc(vtok_ev, 1)
            dve.wait_ge(pair_free, T_MG - 1)
            link(dve.tensor_copy(shst[:, 0, :], zs[:, :, T]))
            dve.tensor_copy(shst[:, 1, :], zs[:, :, W]).then_inc(zs_ready, 1)
            link(dve.memset(zs[:, :, 0:1], 0.0))
            link(dve.tensor_copy(zs[:, :, S0:S0 + 1], par[:, SSH:SSH + ZT].unsqueeze(2)))
            link(dve.memset(oaT[:, :, T:S0], 0.0))
            for h in range(NH):
                dve.wait_ge(flip_mm, h + 1)
                dve.tensor_copy(bias[:, h, :], ps[:, 4 + h % 2, :]).then_inc(flip_ev, 1)
            dve.wait_ge(ada_used, NADA1 + NADA2)
            link(tt(mod[:, 2 * KD:, :], ps[:, 7, 4 * KD:12 * KD].rearrange("p (m s) -> p m s", s=2),
                    par[:, BADA + 2 * KD:BADA + 6 * KD].unsqueeze(2).to_broadcast([P, 4 * KD, 2]), ALU.add))
            scales(1)
            dve.tensor_scalar(omka[:, :], par[:, KAc:KAc + HP], -1.0, 1.0, ALU.mult, ALU.add).then_inc(mod_ready, 1)

            dve.wait_ge(flip_ev, NH)
            link(dve.memset(bias[0:L, :, T - L:T], NEG))
            NJ = 2 * len(TILES)
            with link.loop(HP, 24) as hp:
                def biased(j):
                    t, e, q = j // 2, j % 2, j % 2
                    rows_ = TILES[t][1]
                    dve.wait_ge(s_mm, hp * NJ + (j + 1))
                    if j >= 2:
                        dve.wait_ge(pt_mm, hp * NJ + (j - 1))
                    b = lambda m0, m1: bias[0:rows_, hp * 2 + e, m0:m1]
                    s = lambda a, z: s_sb[0:rows_, q, a:z]
                    if t < TT:
                        n = (t + 1) * P
                        link(tt(s(0, n), ps[0:rows_, q, 0:n], b(T - n, T), ALU.add))
                    else:
                        n = T + TS
                        link(tt(s(0, P), ps[0:rows_, q, 0:P], b(0, P), ALU.add))
                        link(tt(s(P, T), ps[0:rows_, q, P:T], b(0, T - P), ALU.add))
                        link(tt(s(T, n), ps[0:rows_, 6 + q, 0:TS], b(T - P, T - P + TS), ALU.add))
                    dve.tensor_reduce(rsum[0:rows_, q, 1:2], s(0, n), AX, ALU.max, negate=True).then_inc(s_biased, 1)

                def out(j):
                    t, e, q = j // 2, j % 2, j % 2
                    rows_ = TILES[t][1]
                    dve.wait_ge(o_mm, hp * NJ + (j + 1))
                    link(dve.reciprocal(rsum[0:rows_, q, 2:3], rsum[0:rows_, q, 0:1]))
                    sts(otok[0:rows_, t, e * DH:(e + 1) * DH], ps[0:rows_, 4 + q, 0:DH], rsum[0:rows_, q, 2:3], None,
                        ALU.mult).then_inc(o_ev, 1)
                for j in range(NJ + 2):
                    if j >= 2:
                        out(j - 2)
                    if j < NJ:
                        biased(j)

            dve.wait_ge(rw_consts, 1)
            link(dve.memset(E1[:, 0:1], 1.0))

            def shift(t, t_mu):
                z, prev = zs[:, t, 1:W + 1], zs[:, t, 0:W]
                link(tt(bh[:, :], prev, z, ALU.subtract))
                return stt(z, bh[:, :], t_mu, z, ALU.mult, ALU.add)
            for t in (ZT - 2, ZT - 1):
                shift(t, p1(MU + t)).then_inc(zx_done, 1)
                dve.wait_ge(zx_done, t - (ZT - 3))
            with link.loop(ZT - 2, 2) as t:
                link(shift(t, par[:, bass.ds(t + MU, 1)]))
            for m in range(HP):
                sts(kk[:, m, :], zs[:, HP + m, 1:W + 1], p1(KKc + m), None, ALU.mult).then_inc(kkr_done, 1)
            for m in range(HP):
                dve.wait_ge(up_ev, 2 * m + 1)
                link(dve.tensor_tensor_scan(cs[:, m, :], resetm[:, :], cs[:, m, :], 0.0, ALU.mult, ALU.add))
            dve.wait_ge(up_ev, 2 * HP)
            dve.wait_ge(kk_mm, HP)
            link(sts(halves(ss8[:, :]), ps[0:NH, 0:2, 0:H], KK_MIN, None, ALU.max))
            dve.reciprocal(ss8[:, :], ss8[:, :]).then_inc(kkv, 1)
            for m in range(HP):
                dve.wait_ge(kkb_mm, m + 1)
                tt(halves(kk[:, m, :]), halves(kk[:, m, :]), pair(m), ALU.mult)\
                    .then_inc(kk_ready if m < HP - 1 else hp_free, 1)
            dve.wait_ge(kk_ready, HP - 1)
            dve.wait_ge(hp_free, 1)

            with link.loop(HP, 79) as hp:
                z = lambda i: zs[:, hp + i * HP, 1:W + 1]
                hp_par = lambda c: par[:, bass.ds(hp + c, 1)]
                k_hp, a_hp = kk[:, hp, :], aa[:, hp, :]
                link(sts(kh[:, :], a_hp, hp_par(KAc), omka[:, bass.ds(hp, 1)], ALU.mult, ALU.add))
                link(tt(kh[:, :], kh[:, :], z(1), ALU.mult))
                stt(kl[:, :], z(0), hp_par(RKc), kh[:, :], ALU.mult, ALU.mult).then_inc(rk_done, 1)
                dve.wait_ge(exps, hp * 3 + 1)
                link(tt(kt[:, :], k_hp, E1[:, 0:W], ALU.mult))
                for first in (slice(0, T, L), slice(S0, S0 + 1)):
                    link(sts(kt[:, first], kk[:, hp, first], 1.0, None, ALU.mult))
                link(tt(rt[:, :], z(0), E1[:, 1:W + 1], ALU.mult))
                link(tt(bh[:, :], k_hp, a_hp, ALU.mult))
                dve.wait_ge(exps, hp * 3 + 3)
                link(tt(bh[:, :], bh[:, :], E2[:, :], ALU.mult))
                link(tt(kh[:, :], kh[:, :], E2[:, :], ALU.mult))
                dve.wait_ge(bon_mm, hp + 1)
                link(tt(halves(z(1)), pair(0), halves(vst[:, :]), ALU.mult))
                for dst, src in ((bl, bh), (kl, kh)):
                    ends = E1[:, L:T + 1:L].unsqueeze(2).to_broadcast([P, NCH, L])
                    ch = lambda a: a[:, 0:T].rearrange("p (c l) -> p c l", l=L)
                    link(tt(ch(dst), ch(src), ends, ALU.mult))
                    link(dve.tensor_copy(dst[:, T:S0], src[:, T:S0]))
                    if dst is bl:
                        link(sts(dst[:, S0:W], src[:, S0:W], E1[:, W:W + 1], None, ALU.mult))
                    else:
                        sts(dst[:, S0:W], src[:, S0:W], E1[:, W:W + 1], None, ALU.mult).then_inc(ew_done, 1)

                def v_masks(t, q, R):
                    bc = lambda m, n: m[0:R, 0:R].unsqueeze(1).to_broadcast([R, n, R])
                    dve.wait_ge(sc_mm, hp * KS + (t + 1))
                    of = lambda i: ps[0:R, 4 * q + 2:4 * q + 4, i * P:i * P + R]
                    link(tt(CTs[q][0:R, :, 0:R], of(0), bc(strictU, 2), ALU.mult))
                    link(tt(X[q][0:R, :, 0:R], of(1), bc(nM0, 2), ALU.mult))
                    link(tt(BDs[q][0:R, 0:2, 0:R], of(2), bc(inclU, 2), ALU.mult))
                    tt(BDs[q][0:R, 2:4, 0:R], of(3), bc(inclU, 2), ALU.mult).then_inc(masked, 1)
                    link(tt(X[q][0:R, :, 0:R], X[q][0:R, :, 0:R], bc(ident, 2), ALU.add))
                    dve.wait_ge(at_ev, hp * KS + (t + 1))
                    link(tt(XT[q][0:R, :, 0:R], ATs[q][0:R, :, 0:R], bc(nM0T, 2), ALU.mult))
                    tt(XT[q][0:R, :, 0:R], XT[q][0:R, :, 0:R], bc(ident, 2), ALU.add).then_inc(x0_done, 1)

                def v_level_p(t, q, R, lev):
                    s = 2 << lev
                    nb = R // (2 * s)
                    dve.wait_ge(lev_p_mm[q], hp * LEVS[q] + lev_at(t, lev) + 1)
                    if R == P:
                        out = Pb[q][:, :, :].rearrange("p u (b h s) -> p (u b) h s", h=2, s=s)
                        src = bank(q, 2)[:, 0, :].rearrange("p (b s) -> p b s", s=s).unsqueeze(2)\
                            .to_broadcast([P, 2 * nb, 2, s])
                        msk = lmask[:, lev, :, :].rearrange("p u (b h s) -> p (u b) h s", h=2, s=s)
                        tt(out, src, msk, ALU.mult).then_inc(lev_p[q], 1)
                    else:
                        for e in range(2):
                            out = Pb[q][0:R, e, 0:R].rearrange("p (b h s) -> p b h s", h=2, s=s)
                            src = bank(q, 2)[0:R, 0, e * DH:e * DH + R // 2].rearrange("p (b s) -> p b s", s=s)\
                                .unsqueeze(2).to_broadcast([R, nb, 2, s])
                            msk = lmask[0:R, lev, 0, 0:R].rearrange("p (b h s) -> p b h s", h=2, s=s)
                            i = tt(out, src, msk, ALU.mult)
                            if e:
                                i.then_inc(lev_p[q], 1)
                            else:
                                link(i)

                def v_level_x(t, q, R, lev):
                    s = 2 << lev
                    dve.wait_ge(lev_x_mm[q], hp * LEVS[q] + lev_at(t, lev) + 1)
                    last = lev == n_levels(R) - 1
                    if R == P:
                        v = lambda a, h: a[:, :, :].rearrange("p u (b h s) -> p (u b) h s", h=2, s=s)[:, :, h, :]
                        c = lambda o: bank(q, 3)[:, o, :].rearrange("p (b s) -> p b s", s=s)
                        if not last:
                            link(tt(v(X[q], 0), v(X[q], 0), c(0), ALU.subtract))
                        tt(v(XT[q], 1), v(XT[q], 1), c(1), ALU.subtract).then_inc(lev_x[q], 1)
                    else:
                        for e in range(2):
                            v = lambda a, h: a[0:R, e, 0:R].rearrange("p (b h s) -> p b h s", h=2, s=s)[:, :, h, :]
                            c = lambda o: bank(q, 3)[0:R, o, e * DH:e * DH + R // 2].rearrange("p (b s) -> p b s", s=s)
                            if not last:
                                link(tt(v(X[q], 0), v(X[q], 0), c(0), ALU.subtract))
                            i = tt(v(XT[q], 1), v(XT[q], 1), c(1), ALU.subtract)
                            if e:
                                i.then_inc(lev_x[q], 1)
                            else:
                                link(i)

                def v_out(t, q, R):
                    c0 = TILES[t][0]
                    dve.wait_ge(gm_mm, hp * KS + (t + 1))
                    link(tt(zs[:, hp, 1 + c0:1 + c0 + R], bank(q, 2)[:, 0, 0:R], rt[:, c0:c0 + R], ALU.add))
                    nch = 2 if t < TT else 1
                    for c in range(nch):
                        end = c0 + (c + 1) * L if t < TT else W
                        i = stt(MT[:, hp, 2 * t + c, :], dg2[:, :], E1[:, end:end + 1],
                                bank(q, 3 - c)[:, c, 0:DH], ALU.mult, ALU.add)
                        if c == nch - 1:
                            i.then_inc(gm_dve if t < TT else hp_free, 1)
                        else:
                            link(i)
                for tiles in PAIRS:
                    R = TILES[tiles[0]][1]
                    for t in tiles:
                        v_masks(t, t % 2, R)
                    for lev in range(n_levels(R)):
                        for t in tiles:
                            v_level_p(t, t % 2, R, lev)
                        for t in tiles:
                            v_level_x(t, t % 2, R, lev)
                    for t in tiles:
                        v_out(t, t % 2, R)
                dve.wait_ge(hp_free, hp + 2)

            dve.wait_ge(gm_act, HP * KS)
            dve.wait_ge(st_mm, 1)
            link(dve.tensor_copy(SS[:, NCH + 1, :, :], ps[:, 0, 0:HP * DH].rearrange("p (a v) -> p a v", a=HP)))
            dve.tensor_copy(SS[:, 1, :, :], NN[:, :, 0, :]).then_inc(chain_ev, 1)
            for c in range(1, NCH + 1):
                dve.wait_ge(chain_mm, c)
                src = ps[:, 1 + c % 2, 0:HP * DH].rearrange("p (a v) -> p a v", a=HP)
                dst = SS[:, c + 1, :, :] if c < NCH else SS[:, 0, :, :]
                tt(dst, src, NN[:, :, c, :], ALU.add).then_inc(chain_ev, 1)
            for i in range(2):
                dve.wait_ge(fin_mm, i + 1)
                dve.tensor_copy(fin_sb[:, i, :, :], ps[:, 3 + i, 0:HP * DH].rearrange("p (a v) -> p a v", a=HP))\
                   .then_inc(fin_ev, 1)
            for m in range(HP):
                y = zs[:, 2 * HP + m, :]
                dve.wait_ge(y_mm, m + 1)
                q = 2 * (m % 2)
                link(tt(y[:, 1 + L:1 + T], y[:, 1 + L:1 + T], ps[:, q, L:T], ALU.add))
                tt(y[:, 1 + S0:1 + W], y[:, 1 + S0:1 + W], ps[:, q + 1, 0:TS], ALU.add).then_inc(y_done, 1)
            for m in range(HP):
                y = zs[:, 2 * HP + m, 1:W + 1]
                dve.wait_ge(mean_mm, m + 1)
                stt(halves(y), pair(2 + m % 2), -1.0 / DH, halves(y), ALU.mult, ALU.add).then_inc(yc_done, 1)
            dve.wait_ge(var_mm, HP)
            link(sts(halves(ss8[:, :]), ps[0:NH, 0:2, 0:H], 1.0 / DH, GN_EPS, ALU.mult, ALU.add))
            dve.reciprocal(ss8[:, :], ss8[:, :]).then_inc(var8, 1)
            for m in range(HP):
                y = zs[:, 2 * HP + m, 1:W + 1]
                o = (kt, rt)[m % 2]
                dve.wait_ge(gate_mm, m + 1)
                if m >= 2:
                    dve.wait_ge(ob_done, m - 1)
                link(tt(halves(o[:, :]), pair(2 * (m % 2)), halves(y), ALU.mult))
                link(sts(o[:, :], o[:, :], p1(GG + m), p1(GB + m), ALU.mult, ALU.add))
                link(tt(o[:, :], o[:, :], zs[:, HP + m, 1:W + 1], ALU.add))
                tt(halves(o[:, :]), halves(o[:, :]), pair(2 * (m % 2) + 1), ALU.mult).then_inc(ob_f32, 1)
                dve.wait_ge(obh_done, m + 1)
                tt(obl[:, m, :], o[:, :], obh[:, m, :].bitcast(F32), ALU.subtract).then_inc(ob_done, 1)
            dve.wait_ge(oah_done, 1)
            tt(oal[:, :, :], oaT[:, :, :], oah[:, :, :].bitcast(F32), ALU.subtract).then_inc(ob_done, 1)

            with dve.Fori(0, D // UW // 2) as g2:
                for g in range(2):
                    for m in range(2):
                        n = g2 * 16 + (T_MG + 8 * g + 4 + 2 * m)
                        dve.wait_ge(tile_mm, g2 * 10 + (M_MG + 5 * g + 2 * m + 3))
                        dve.wait_ge(pair_free, n - 1)
                        tt(halves(mt[:, 0, :]), pair(0), halves(sg1[:, m, :]), ALU.mult).then_inc(pair_free, 1)
                        if m == 0:
                            dve.wait_ge(tile_mm, g2 * 10 + (M_MG + 5 * g + 4))
                        else:
                            dve.wait_ge(unit_mm, g2 * 6 + (U_MG + 3 * g + 3))
                        tt(halves(mt[:, 1, :]), pair(1), halves(sg2[:, m, :]), ALU.mult).then_inc(pair_free, 1)
                        dve.wait_ge(pair_free, n + 1)
                        tt(mt[:, 0, :], mt[:, 0, :], mt[:, 1, :], ALU.add).then_inc(mg_f32, 1)
                        k = g2 * 4 + (2 * g + m)
                        dve.wait_ge(mgh_done, k + 1)
                        tt(mgl[:, k, :], mt[:, 0, :], mgh[:, k, :].bitcast(F32), ALU.subtract).then_inc(mg_done, 1)
                        dve.wait_ge(mg_done, k + 1)

            def residual(q, k, gt):
                g = lambda s: mod[:, bass.ds(k + gt, 1), s:s + 1].rearrange("p a b -> p (a b)")
                xa = xT[:, k, :]
                link(stt(xa[:, 0:H], ps[:, 2 * q, 0:H], g(0), xa[:, 0:H], ALU.mult, ALU.add))
                link(stt(xa[:, H:S0], ps[:, 2 * q + 1, 0:S0 - H], g(0), xa[:, H:S0], ALU.mult, ALU.add))
                return stt(xa[:, S0:W], ps[:, 2 * q + 1, S0 - H:H], g(1), xa[:, S0:W], ALU.mult, ALU.add)
            dve.wait_ge(x_back, 16)
            with link.loop(KD // 2, 4) as k2:
                for j in range(2):
                    if j == 0:
                        dve.wait_ge(tile_mm, k2 + (M_WO + 1))
                    else:
                        dve.wait_ge(unit_mm, k2 + (U_WO + 1))
                    residual(j, k2 * 2 + j, GT1).then_inc(pair_free, 1)
            dve.wait_ge(pair_free, T_UP - 1)
            norm(1, SH2, SCL2)

            def ffn(i, s):
                n = i * 2 + T_UP
                dve.wait_ge(pair_free, n)
                dve.wait_ge(unit_mm, i + (U_UP + 1))
                tt(halves(ff_a[:, :]), pair(1), halves(ff_g[:, :]), ALU.mult).then_inc(pair_free, 1)
                dve.wait_ge(ah_done, i + 1)
                tt(al[:, i, :], ff_a[:, :], ah[:, i, :].bitcast(F32), ALU.subtract).then_inc(act_done, 1)
                dve.wait_ge(act_done, i + 1)
            two_by_two(dve, 0, NUP, ffn)
            with link.loop(KD // 2, 4) as k2:
                for j in range(2):
                    dve.wait_ge(unit_mm, k2 * 4 + (U_DN + 2 * j + 2))
                    residual(j, k2 * 2 + j, GT2).then_inc(pair_free, 1)

            for t, (_, rows_) in enumerate(TILES):
                q = t % 2
                dve.wait_ge(ysq_done, t + 1)
                c = stat[0:rows_, t:t + 1]
                link(sts(c, c, 1.0 / D, RMS_EPS, ALU.mult, ALU.add))
                dve.reciprocal(c, c).then_inc(yv, 1)
                dve.wait_ge(yr, t + 1)
                if t >= 2:
                    dve.wait_ge(y_out[q], 16 * (t // 2))
                if t == 0:
                    dve.wait_ge(gf_in, 16)
                v = lambda a: a.rearrange("p (b c) -> p b c", b=2)
                stt(v(y_sb[0:rows_, q, :]), ps[0:rows_, 2 * q:2 * q + 2, :], c, v(gf_row[0:rows_, :]),
                    ALU.mult, ALU.mult).then_inc(yt_done, 1)

        @block.tensor
        def _(pe):
            def mm(out, lhsT, rhs, start=True, stop=True):
                return pe.matmul(out, lhsT, rhs, start=start, stop=stop)

            def pe_wait(t, sem_, value):
                if t == TT:
                    wait_alone(pe, sem_, value)
                else:
                    pe.wait_ge(sem_, value)

            pe.wait_ge(consts_made, 3)
            pe.wait_ge(rows_in, 16 * 14)
            pe.transpose(ps[:, 0, 0:N1], rows1[:, :], ident[0:N1, 0:N1])
            pe.transpose(ps[:, 0, P:P + N2], rows2[:, :], ident[0:N2, 0:N2]).then_inc(tile_mm, 1)
            pe.wait_ge(x_in, 32)
            for t, (_, rows_) in enumerate(TILES):
                if t == 1:
                    pe.wait_ge(par_ready, 1)
                if t >= 2:
                    pe.wait_ge(pair_free, t - 1)
                q = (t + 1) % 2
                for k in range(KD):
                    src = (xtok[:, t, :] if t < TT else xtok_s[:, :])[:, k * P:(k + 1) * P]
                    o = ps[:, 2 * q + k // 4, (k % 4) * P:(k % 4) * P + rows_]
                    i = pe.transpose(o, src, ident[0:rows_, 0:rows_])
                i.then_inc(tile_mm, 1)

            def ada(i, s, r):
                pe.wait_ge(raw_in[s], r * 16 + (32 - 16 * s))
                w = w_raw[:, s, :].rearrange("p (k c) -> p k c", k=KD)
                for m in range(2):
                    o = ps[:, 7, bass.ds(i * 4 + 2 * m, 2)]
                    for k in range(KD):
                        ins = mm(o, w[:, k, m * P:(m + 1) * P], sc2[:, k, :], k == 0, k == KD - 1)
                ins.then_inc(ada_used, 1)
            pe.wait_ge(sc2_ready, 1)
            two_by_two(pe, 0, NADA1, lambda i, s: ada(i, s, i))

            def sum_squares(i):
                for k in range(KD):
                    pe.wait_ge(sq_done, i * KD + k + 1)
                    for h in range(2):
                        ins = mm(ps[:, 4 + h, 0:H], ones[:, :], sq_a[:, k % 2, h * H:(h + 1) * H], k == 0, k == KD - 1)
                    ins.then_inc(ss_mm, 1)
            sum_squares(0)

            def product(n, q, s, terms, first=True, last=True):
                if first:
                    pe.wait_ge(pair_free, n - 2)
                for i, (c, xh, xl) in enumerate(terms):
                    for j, (w, x) in enumerate(((w_hi, xh), (w_hi, xl), (w_lo, xh))):
                        for h in range(2):
                            ins = mm(ps[:, 2 * q + h, 0:H], w[:, s, c:c + P], x[:, h * H:(h + 1) * H],
                                     first and i == 0 and j == 0, last and i == len(terms) - 1 and j == 2)
                return ins

            def unit(i, s, n0, tiles):
                pe.wait_ge(lo_done, i + 1)
                for j, terms in enumerate(tiles):
                    last = j == len(tiles) - 1
                    product(n0 + j, j % 2, s, terms).then_inc(unit_mm if last else tile_mm, 1)

            def terms(xh, xl, m, k0=0, n=KD):
                return [((k0 + k) * UW + m * P, xh[:, k, :], xl[:, k, :]) for k in range(n)]

            pe.wait_ge(h_done, KD)
            project = lambda i, s: unit(i, s, i * 2 + T_QKV, [terms(hh, hl, m) for m in range(2)])
            two_by_two(pe, 0, NQKV + NZS, project)

            pe.wait_ge(pair_free, T_MG - 1)
            for t, (c0, rows_) in enumerate(TILES):
                if t >= 2:
                    pe.wait_ge(ktok_ev, t - 1)
                    pe.wait_ge(vtok_ev, t - 1)
                for i, done in enumerate((ktok_mm, vtok_mm)):
                    for f in range(HP):
                        ins = pe.transpose(ps[0:rows_, 2 * i + t % 2, f * P:(f + 1) * P],
                                           qkvT[:, (1 + i) * HP + f, c0:c0 + rows_], ident[:, :])
                    ins.then_inc(done, 1)
            pe.wait_ge(bias_in, 16)
            for h in range(NH):
                if h >= 2:
                    pe.wait_ge(flip_ev, h - 1)
                mm(ps[:, 4 + h % 2, :], anti[:, :], bias[:, h, :]).then_inc(flip_mm, 1)
            pe.wait_ge(zs_ready, 1)
            pe.transpose(ps[0:2 * ZT, 6, 0:P], shst[:, :, :].rearrange("p s t -> p (s t)"), ident[:, :]).then_inc(shift_mm, 1)
            two_by_two(pe, 0, NADA2, lambda i, s: ada(i + NADA1, 1 - s, i + (NADA1 + U_MG)))

            NJ = 2 * len(TILES)
            pe.wait_ge(vtok_ev, KS)
            pe.wait_ge(shift_st, 1)
            pe.wait_ge(mod_ready, 1)
            with pe.Fori(0, HP) as hp:
                pe.wait_ge(staged, hp * 4 + 4)

                def scores(j):
                    t, e = j // 2, j % 2
                    c0, rows_ = TILES[t]
                    part = slice(e * DH, (e + 1) * DH)
                    if j >= 2:
                        pe_wait(t, s_biased, hp * NJ + (j - 1))
                    q = qs[part, c0:c0 + rows_]
                    if t < TT:
                        mm(ps[:, e, 0:c0 + P], q, ks[part, 0:c0 + P]).then_inc(s_mm, 1)
                    else:
                        wait_alone(pe, kct_ev, hp + 1)
                        mm(ps[0:rows_, e, :], q, kcT[part, :])
                        mm(ps[0:rows_, 6 + e, 0:rows_], q, ks[part, c0:c0 + rows_]).then_inc(s_mm, 1)

                def pt_count(j):
                    return hp * (NJ + 2) + (j + 1 + max(0, j - 2 * TT + 1))

                def transposes(j):
                    t, e = j // 2, j % 2
                    rows_ = TILES[t][1]
                    pe_wait(t, p_done, hp * NJ + (j + 1))
                    if j >= 2:
                        pe_wait(t, pt_ev, pt_count(j - 2))
                    nb = t + 1 if t < TT else TT
                    for b in range(nb):
                        ins = pe.transpose(ps[:, 2 + e, b * rows_:(b + 1) * rows_], s_sb[0:rows_, e, b * P:(b + 1) * P],
                                           ident[0:rows_, 0:rows_])
                    if t == TT:
                        ins = pe.transpose(ps[0:TS, 2 + e, nb * TS:(nb + 1) * TS], s_sb[0:TS, e, T:T + TS],
                                           ident[0:TS, 0:TS])
                    ins.then_inc(pt_mm, 1)

                def values(j):
                    t, e = j // 2, j % 2
                    rows_ = TILES[t][1]
                    cols = slice(e * DH, (e + 1) * DH)
                    pe.wait_ge(pt_ev, pt_count(j))
                    if j >= 2:
                        pe.wait_ge(o_ev, hp * NJ + (j - 1))
                    o = ps[0:rows_, 4 + e, 0:DH]
                    if t < TT:
                        for b in range(t + 1):
                            ins = mm(o, pt_sb[:, e, b * P:(b + 1) * P], vs[:, b, cols], b == 0, b == t)
                    else:
                        pe.wait_ge(vc_in, hp * 16 + 16)
                        for b in range(TT):
                            mm(o, pt_sb[:, e, b * TS:(b + 1) * TS], vcs[:, b, cols], b == 0, False)
                        ins = mm(o, pt_sb[0:TS, e, TT * TS:(TT + 1) * TS], vs[0:TS, TT, cols], False, True)
                    ins.then_inc(o_mm, 1)
                for j in range(NJ + 2):
                    if j < NJ:
                        scores(j)
                    if j == 3:
                        pe.wait_ge(kc_in, hp * 16 + 16)
                        for b in range(TT):
                            ins = pe.transpose(ps[:, 7, b * P:(b + 1) * P], kc_raw[:, b, :], ident[:, :])
                        ins.then_inc(kct_mm, 1)
                    if 1 <= j <= NJ:
                        transposes(j - 1)
                    if j >= 2:
                        values(j - 2)
                pe.wait_ge(o_ev, hp * NJ + NJ)
                for t, (_, rows_) in enumerate(TILES):
                    o = ps[:, 6, t * P:(t + 1) * P] if t < TT else ps[:, 7, 0:TS]
                    ins = pe.transpose(o, otok[0:rows_, t, :], ident[0:rows_, 0:rows_])
                ins.then_inc(ot_mm, 1)

            pe.wait_ge(rw_consts, 1)
            pe.wait_ge(ot_ev, HP)
            pe.wait_ge(up_in, 48)
            pe.wait_ge(td_done, 1)
            for m in range(HP):
                for j in range(2):
                    n = 2 * m + j
                    if n >= 4:
                        pe.wait_ge(up_ev, n - 3)
                    part = slice(j * DH, (j + 1) * DH)
                    for h in range(2):
                        ins = mm(ps[:, 2 * (n % 4) + h, 0:H], wup[part, m * P:(m + 1) * P],
                                 zs[part, ZT - 2, 1 + h * H:1 + (h + 1) * H])
                    ins.then_inc(up_mm, 1)
            pe.wait_ge(up_ev, 2 * HP)
            for m in range(HP):
                pe.wait_ge(kksq, m + 1)
                for h in range(2):
                    ins = mm(ps[0:NH, h, 0:H], ind[:, m, :], (kt, rt)[m % 2][:, h * H:(h + 1) * H], m == 0, m == HP - 1)
                ins.then_inc(kk_mm, 1)
            pe.wait_ge(rkk, 1)
            for m in range(HP):
                for h in range(2):
                    ins = mm(ps[:, 2 * m + h, 0:H], indT[:, m, :], ss8[:, h * H:(h + 1) * H])
                ins.then_inc(kkb_mm, 1)

            with pe.Fori(0, HP) as hp:
                pe.wait_ge(rk_done, hp + 1)
                pe.wait_ge(exps, hp * 3 + 3)
                for h in range(2):
                    ins = mm(ps[:, h, 0:H], bones[:, :], kl[:, h * H:(h + 1) * H])
                ins.then_inc(bon_mm, 1)
                pe.wait_ge(ew_done, hp + 1)
                part = [slice(0, DH), slice(DH, P)]

                def p_scores(t, q, R):
                    c = slice(TILES[t][0], TILES[t][0] + R)
                    if t >= 2:
                        pe_wait(t, gm_dve, hp * TT + (t - 1))
                        pe_wait(t, gm_act, hp * KS + (t - 1))
                    for e in range(2):
                        mm(bank(q, e)[0:R, 0, 0:R], bh[part[e], c], kt[part[e], c])
                        for i, (a, b) in enumerate(((kh, kt), (kt, bh), (bh, rt), (kh, rt))):
                            mm(bank(q, 2 + e)[0:R, i, 0:R], a[part[e], c], b[part[e], c])
                    pe.transpose(bank(q, 0)[0:R, 1, :], kt[:, c], ident[:, :])
                    for i, x in enumerate((bl, kl, vst)):
                        ins = pe.transpose(bank(q, 1)[0:R, 1 + i, :], x[:, c], ident[:, :])
                    ins.then_inc(sc_mm, 1)

                def p_cv(t, q, R):
                    pe_wait(t, masked, hp * KS + (t + 1))
                    pe_wait(t, tk_ev, hp * KS + (t + 1))
                    for e in range(2):
                        ins = mm(bank(q, 0)[0:R, 0, part[e]], CTs[q][0:R, e, 0:R], tk[q][0:R, 2, part[e]])
                    ins.then_inc(cv_mm, 1)

                def half(a, R, s, h):
                    return a.rearrange("p (b h s) -> p b h s", h=2, s=s)[:, :, h, :]

                def p_level_p(t, q, R, lev):
                    s = 2 << lev
                    if lev == 0:
                        pe_wait(t, x0_done, hp * KS + (t + 1))
                    else:
                        pe_wait(t, lev_x[q], hp * LEVS[q] + lev_at(t, lev))
                    for e in range(2):
                        ins = mm(bank(q, 2)[0:R, 0, e * DH:e * DH + R // 2], ATs[q][0:R, e, 0:R],
                                 half(X[q][0:R, e, 0:R], R, s, 0))
                    ins.then_inc(lev_p_mm[q], 1)

                def p_level_x(t, q, R, lev):
                    s = 2 << lev
                    pe_wait(t, lev_p[q], hp * LEVS[q] + lev_at(t, lev) + 1)
                    for e in range(2):
                        if lev < n_levels(R) - 1:
                            mm(bank(q, 3)[0:R, 0, e * DH:e * DH + R // 2], XT[q][0:R, e, 0:R],
                               half(Pb[q][0:R, e, 0:R], R, s, 0))
                        ins = mm(bank(q, 3)[0:R, 1, e * DH:e * DH + R // 2], Pb[q][0:R, e, 0:R],
                                 half(XT[q][0:R, e, 0:R], R, s, 1))
                    ins.then_inc(lev_x_mm[q], 1)

                def p_wu(t, q, R):
                    pe_wait(t, lev_x[q], hp * LEVS[q] + lev_at(t, n_levels(R)))
                    pe_wait(t, cv_ev, hp * KS + (t + 1))
                    for e in range(2):
                        ins = mm(bank(q, 1)[0:R, e, :], XT[q][0:R, e, 0:R], KC[q][0:R, e, :])
                    ins.then_inc(wu_mm, 1)

                def p_out(t, q, R):
                    pe.wait_ge(wu_ev, hp * KS + (t + 1))
                    w_, b_, k_ = WU[q], tk[q], BDs[q]
                    for e in range(2):
                        mm(bank(q, 2)[part[e], 0, 0:R], w_[0:R, e, 0:DH], k_[0:R, e, 0:R])
                        mm(bank(q, 0)[part[e], 0, 0:R], b_[0:R, 2, part[e]], k_[0:R, 2 + e, 0:R], True, False)
                        mm(bank(q, 0)[part[e], 0, 0:R], w_[0:R, e, DH:P], k_[0:R, e, 0:R], False, True)
                        for c in range(2 if R == P else 1):
                            r = slice(c * L, c * L + min(R, L))
                            om, on = [bank(q, i - c)[part[e], c, 0:DH] for i in (3, 1)]
                            mm(om, w_[r, e, 0:DH], b_[r, 0, part[e]])
                            mm(on, b_[r, 1, part[e]], b_[r, 2, part[e]], True, False)
                            ins = mm(on, b_[r, 0, part[e]], w_[r, e, DH:P], False, True)
                    ins.then_inc(gm_mm, 1)
                for tiles in PAIRS:
                    R = TILES[tiles[0]][1]
                    for t in tiles:
                        p_scores(t, t % 2, R)
                    for t in tiles:
                        p_cv(t, t % 2, R)
                    for lev in range(n_levels(R)):
                        for t in tiles:
                            p_level_p(t, t % 2, R, lev)
                        for t in tiles:
                            p_level_x(t, t % 2, R, lev)
                    for t in tiles:
                        p_wu(t, t % 2, R)
                    for t in tiles:
                        p_out(t, t % 2, R)

            part = [slice(0, DH), slice(DH, P)]
            pe.wait_ge(hp_free, HP + 1)
            pe.wait_ge(gm_act, HP * KS)
            pe.wait_ge(st_in, 16)

            def flip(b, src, done):
                for a in range(HP):
                    for e in range(2):
                        ins = mm(ps[part[e], b, a * DH:(a + 1) * DH], src[part[e], a, :], ident[part[e], part[e]])
                ins.then_inc(done, 1)
            flip(0, stv, st_mm)
            for c in range(1, NCH + 1):
                pe.wait_ge(chain_ev, c)
                for a in range(HP):
                    for e in range(2):
                        ins = mm(ps[part[e], 1 + c % 2, a * DH:(a + 1) * DH], MT[part[e], a, c, :],
                                 SS[part[e], c if c < NCH else NCH + 1, a, :])
                ins.then_inc(chain_mm, 1)
            flip(3, SS[:, NCH, :, :], fin_mm)
            pe.wait_ge(chain_ev, NCH + 1)
            flip(4, SS[:, 0, :, :], fin_mm)
            pe.wait_ge(fin_ev, 2)
            for m in range(HP):
                q = 2 * (m % 2)
                if m >= 2:
                    pe.wait_ge(y_done, m - 1)
                for e in range(2):
                    for c in range(1, NCH):
                        mm(ps[part[e], q, c * L:(c + 1) * L], SS[part[e], c, m, :],
                           zs[part[e], m, 1 + c * L:1 + (c + 1) * L])
                    ins = mm(ps[part[e], q + 1, 0:TS], SS[part[e], NCH + 1, m, :], zs[part[e], m, 1 + S0:1 + W])
                ins.then_inc(y_mm, 1)
            for m in range(HP):
                pe.wait_ge(y_done, m + 1)
                if m >= 2:
                    pe.wait_ge(yc_done, m - 1)
                for h in range(2):
                    ins = mm(ps[:, 4 + 2 * (m % 2) + h, 0:H], bones[:, :], zs[:, 2 * HP + m, 1 + h * H:1 + (h + 1) * H])
                ins.then_inc(mean_mm, 1)
            for m in range(HP):
                pe.wait_ge(ysq, m + 1)
                for h in range(2):
                    ins = mm(ps[0:NH, h, 0:H], ind[:, m, :], (kt, rt)[m % 2][:, h * H:(h + 1) * H], m == 0, m == HP - 1)
                ins.then_inc(var_mm, 1)
            pe.wait_ge(rs8, 1)
            for m in range(HP):
                if m >= 2:
                    pe.wait_ge(ob_f32, m - 1)
                b = 4 * (m % 2)
                for h in range(2):
                    mm(ps[:, b + h, 0:H], indT[:, m, :], ss8[:, h * H:(h + 1) * H])
                for h in range(2):
                    ins = mm(ps[:, b + 2 + h, 0:H], wrg[:, m * P:(m + 1) * P], zs[:, ZT - 1, 1 + h * H:1 + (h + 1) * H])
                ins.then_inc(gate_mm, 1)

            pe.wait_ge(ob_done, HP + 1)
            with pe.Fori(0, D // UW // 2) as g2:
                for j in range(6):
                    i = g2 * 6 + (U_MG + j)
                    n0 = g2 * 16 + (T_MG + 8 * (j // 3) + 2 * (j % 3))
                    if j % 3 < 2:
                        unit(i, (U_MG + j) % 2, n0, [terms(hh, hl, m) for m in range(2)])
                    else:
                        unit(i, (U_MG + j) % 2, n0, [terms(xh, xl, m, k0, HP) for m in range(2)
                                                     for xh, xl, k0 in ((oah, oal, 0), (obh, obl, HP))])
            pe.wait_ge(mg_done, KD)
            two_by_two(pe, U_WO, NWO, lambda i, s: unit(i, s, i * 2 + (T_WO - 2 * U_WO), [
                terms(mgh, mgl, m) for m in range(2)]))
            sum_squares(1)

            pe.wait_ge(h_done, 2 * KD)
            two_by_two(pe, U_UP, NUP, lambda i, s: unit(i, s, i * 2 + (T_UP - 2 * U_UP), [
                terms(hh, hl, m) for m in (1, 0)]))
            pe.wait_ge(act_done, NUP)
            with pe.Fori(0, KD // 2) as k2:
                for j in range(2):
                    for part_ in range(2):
                        i = k2 * 4 + (U_DN + 2 * j + part_)
                        pe.wait_ge(lo_done, i + 1)
                        x = [(k * P, ah[:, part_ * KDN + k, :], al[:, part_ * KDN + k, :]) for k in range(KDN)]
                        product(k2 * 2 + (T_DN + j), j, (U_DN + part_) % 2, x, part_ == 0, part_ == 1)\
                            .then_inc(unit_mm, 1)

            pe.wait_ge(pair_free, T_Y - 1)
            for t, (c0, rows_) in enumerate(TILES):
                if t >= 2:
                    pe.wait_ge(yt_done, t - 1)
                for k in range(KD):
                    ins = pe.transpose(ps[0:rows_, 2 * (t % 2) + k // 4, (k % 4) * P:(k % 4 + 1) * P],
                                       xT[:, k, c0:c0 + rows_], ident[:, :])
                ins.then_inc(yt_mm, 1)


INS = ["x_prompt", "x_sample", "cache_attn_k", "cache_attn_v", "state_wkv", "state_shift", "c_prompt", "c_sample",
       "w_ada", "b_ada", "g_norm", "w_in", "rel_bias", "mu", "w0", "w_decay_up", "a0", "w_iclr_up", "w_rg_up",
       "k_k", "k_a", "r_k", "gn_g", "gn_b", "w_out_attn", "w_out_rwkv", "w_out", "w_ffn_in", "w_ffn_out", "g_final"]


def kernel(**inputs):
    import numpy as np
    import concourse.bacc as bacc
    from concourse.bass_utils import run_bass_kernel_spmd

    nc = bacc.Bacc("TRN2", target_bir_lowering=False, num_devices=1)
    arrays, args = {}, []
    for name in INS:
        a = np.ascontiguousarray(inputs[name])
        arrays[f"in_{name}"] = a
        args.append(nc.dram_tensor(f"in_{name}", a.shape, mybir.dt.from_np(a.dtype), kind="ExternalInput").ap())
    T, D = inputs["x_prompt"].shape[1:]
    TS = inputs["x_sample"].shape[1]
    SC = inputs["mu"].shape[1]
    outs = [(1, T, D), (1, TS, D), (1, 1, T, 8, 64), (1, 1, T, 8, 64), (1, 1, 8, 64, 64), (1, 1, SC),
            (1, 1, TS, 8, 64), (1, 1, TS, 8, 64), (1, 1, 8, 64, 64), (1, 1, SC)]
    for i, shape in enumerate(outs):
        args.append(nc.dram_tensor(f"out_{i}", shape, F32, kind="ExternalOutput").ap())
    build(nc, *args)
    r = run_bass_kernel_spmd(nc, [arrays], core_ids=[0])
    return tuple(r.results[0][f"out_{i}"] for i in range(len(outs)))
```
